# Optimizing a Trainium2 kernel written in Bass

```python
import jax, jax.numpy as jnp
from jax import lax
import numpy as np
import math

D_MODEL = 1024
BATCH = 1
SEQ = 512
DEPTH = 1

PLE_DIM = 256
MLA_HEADS = 8
QK_NOPE_DIM = 64
QK_ROPE_DIM = 32
V_HEAD_DIM = 64
Q_LORA_RANK = 384
KV_LORA_RANK = 256
ROPE_THETA = 10000.0
Q_BLOCK = 128
CONV_CHANNELS = 512
CONV_WIDTH = 31
MLA_WIDTH = MLA_HEADS * V_HEAD_DIM
D_MIX = MLA_WIDTH + CONV_CHANNELS
IN_PROJ_DIM = Q_LORA_RANK + KV_LORA_RANK + QK_ROPE_DIM + 2 * CONV_CHANNELS
D_FF = 2816
FFN_CONV_WIDTH = 3
NORM_EPS = 1e-6


def rms_norm(x, g):
    xf = x.astype(jnp.float32)
    y = xf * lax.rsqrt(jnp.mean(xf * xf, axis=-1, keepdims=True) + NORM_EPS)
    return (y * g.astype(jnp.float32)).astype(x.dtype)

def layer_norm(x, g, b):
    xf = x.astype(jnp.float32)
    mu = jnp.mean(xf, axis=-1, keepdims=True)
    xc = xf - mu
    y = xc * lax.rsqrt(jnp.mean(xc * xc, axis=-1, keepdims=True) + NORM_EPS)
    return (y * g.astype(jnp.float32) + b.astype(jnp.float32)).astype(x.dtype)

def causal_depthwise_conv(x, w, b):
    k = w.shape[0]
    out = lax.conv_general_dilated(
        x, w[:, None, :].astype(x.dtype), window_strides=(1,), padding=((k - 1, 0),),
        dimension_numbers=('NWC', 'WIO', 'NWC'), feature_group_count=x.shape[-1])
    return out + b.astype(x.dtype)

def apply_rope(x, cos, sin):
    x1, x2 = jnp.split(x, 2, axis=-1)
    return jnp.concatenate([x1 * cos - x2 * sin, x1 * sin + x2 * cos], axis=-1)

def causal_mla_attention(q_nope, q_rope, k_nope, k_rope, v):
    b, s, h, _ = q_nope.shape
    nb = s // Q_BLOCK
    scale = (QK_NOPE_DIM + QK_ROPE_DIM) ** -0.5
    k_idx = jnp.arange(s)

    def to_blocks(t):
        return jnp.moveaxis(t.reshape(b, nb, Q_BLOCK, *t.shape[2:]), 1, 0)

    def block(args):
        qn, qr, start = args
        sc = (jnp.einsum('bqhd,bkhd->bhqk', qn, k_nope, preferred_element_type=jnp.float32)
              + jnp.einsum('bqhr,bkr->bhqk', qr, k_rope, preferred_element_type=jnp.float32)) * scale
        q_idx = start + jnp.arange(Q_BLOCK)
        sc = jnp.where(k_idx[None, :] <= q_idx[:, None], sc, -jnp.inf)
        pr = jax.nn.softmax(sc, axis=-1).astype(v.dtype)
        return jnp.einsum('bhqk,bkhd->bqhd', pr, v)

    starts = jnp.arange(nb) * Q_BLOCK
    out = lax.map(block, (to_blocks(q_nope), to_blocks(q_rope), starts))
    return jnp.moveaxis(out, 0, 1).reshape(b, s, h * V_HEAD_DIM)

def hybrid_mixer(xn, cos, sin, w_in, g_q_a, w_q_b, g_kv_a, w_kv_b,
                 conv_w, conv_b, conv_ln_g, conv_ln_b, w_o):
    b, s, _ = xn.shape
    proj = xn @ w_in
    o1 = Q_LORA_RANK
    o2 = o1 + KV_LORA_RANK
    o3 = o2 + QK_ROPE_DIM
    q_a, kv_a, k_rope, conv_in = jnp.split(proj, [o1, o2, o3], axis=-1)
    q = (rms_norm(q_a, g_q_a) @ w_q_b).reshape(b, s, MLA_HEADS, QK_NOPE_DIM + QK_ROPE_DIM)
    q_nope, q_rope = jnp.split(q, [QK_NOPE_DIM], axis=-1)
    kv = (rms_norm(kv_a, g_kv_a) @ w_kv_b).reshape(b, s, MLA_HEADS, QK_NOPE_DIM + V_HEAD_DIM)
    k_nope, v = jnp.split(kv, [QK_NOPE_DIM], axis=-1)
    q_rope = apply_rope(q_rope, cos[:, :, None, :], sin[:, :, None, :])
    k_rope = apply_rope(k_rope, cos, sin)
    attn = causal_mla_attention(q_nope, q_rope, k_nope, k_rope, v)
    a, gate = jnp.split(conv_in, 2, axis=-1)
    c = a * jax.nn.sigmoid(gate)
    c = causal_depthwise_conv(c, conv_w, conv_b)
    c = jax.nn.silu(layer_norm(c, conv_ln_g, conv_ln_b))
    return jnp.concatenate([attn, c], axis=-1) @ w_o

def conv_gated_ffn(xn, w_gate, w_up, dw_w, dw_b, w_down):
    g = causal_depthwise_conv(xn @ w_gate, dw_w, dw_b)
    return (jax.nn.gelu(g, approximate=True) * (xn @ w_up)) @ w_down

def first_inputs(seed: int = 0) -> dict:
    key = jax.random.key(seed)
    ks = iter(jax.random.split(key, 40))

    def w(shape, fan_in):
        return jax.random.normal(next(ks), shape, jnp.float32) * fan_in ** -0.5

    def gain(shape):
        return 1.0 + 0.05 * jax.random.normal(next(ks), shape, jnp.float32)

    def bias(shape):
        return 0.01 * jax.random.normal(next(ks), shape, jnp.float32)

    L = DEPTH
    x = jax.random.normal(next(ks), (BATCH, SEQ, D_MODEL), jnp.float32)
    p = jax.random.normal(next(ks), (DEPTH, BATCH, SEQ, PLE_DIM), jnp.float32)
    positions = jnp.broadcast_to(jnp.arange(SEQ, dtype=jnp.int32)[None, :], (BATCH, SEQ))
    return {
        "x": x,
        "p": p,
        "positions": positions,
        "g_mix_pre": gain((L, D_MODEL)),
        "w_in": w((L, D_MODEL, IN_PROJ_DIM), D_MODEL),
        "g_q_a": gain((L, Q_LORA_RANK)),
        "w_q_b": w((L, Q_LORA_RANK, MLA_HEADS * (QK_NOPE_DIM + QK_ROPE_DIM)), Q_LORA_RANK),
        "g_kv_a": gain((L, KV_LORA_RANK)),
        "w_kv_b": w((L, KV_LORA_RANK, MLA_HEADS * (QK_NOPE_DIM + V_HEAD_DIM)), KV_LORA_RANK),
        "conv_w": w((L, CONV_WIDTH, CONV_CHANNELS), CONV_WIDTH),
        "conv_b": bias((L, CONV_CHANNELS)),
        "conv_ln_g": gain((L, CONV_CHANNELS)),
        "conv_ln_b": bias((L, CONV_CHANNELS)),
        "w_o": w((L, D_MIX, D_MODEL), D_MIX),
        "g_mix_post": gain((L, D_MODEL)),
        "g_ffn_pre": gain((L, D_MODEL)),
        "w_ffn_gate": w((L, D_MODEL, D_FF), D_MODEL),
        "w_ffn_up": w((L, D_MODEL, D_FF), D_MODEL),
        "ffn_dw_w": w((L, FFN_CONV_WIDTH, D_FF), FFN_CONV_WIDTH),
        "ffn_dw_b": bias((L, D_FF)),
        "w_ffn_down": w((L, D_FF, D_MODEL), D_FF),
        "g_ffn_post": gain((L, D_MODEL)),
        "w_ple_proj": w((L, PLE_DIM, D_MODEL), PLE_DIM),
        "g_ple": gain((L, D_MODEL)),
        "w_ple_gate": w((L, D_MODEL, D_MODEL), D_MODEL),
    }

def first_block(x, p, positions, g_mix_pre, w_in, g_q_a, w_q_b, g_kv_a, w_kv_b,
              conv_w, conv_b, conv_ln_g, conv_ln_b, w_o, g_mix_post, g_ffn_pre,
              w_ffn_gate, w_ffn_up, ffn_dw_w, ffn_dw_b, w_ffn_down, g_ffn_post,
              w_ple_proj, g_ple, w_ple_gate):
    inv_freq = ROPE_THETA ** (-jnp.arange(0, QK_ROPE_DIM, 2, dtype=jnp.float32) / QK_ROPE_DIM)
    ang = positions.astype(jnp.float32)[..., None] * inv_freq
    cos = jnp.cos(ang).astype(x.dtype)
    sin = jnp.sin(ang).astype(x.dtype)

    h = x
    for i in range(DEPTH):
        mix = hybrid_mixer(rms_norm(h, g_mix_pre[i]), cos, sin, w_in[i], g_q_a[i], w_q_b[i],
                           g_kv_a[i], w_kv_b[i], conv_w[i], conv_b[i], conv_ln_g[i],
                           conv_ln_b[i], w_o[i])
        h = h + rms_norm(mix, g_mix_post[i])
        ffn = conv_gated_ffn(rms_norm(h, g_ffn_pre[i]), w_ffn_gate[i], w_ffn_up[i],
                             ffn_dw_w[i], ffn_dw_b[i], w_ffn_down[i])
        h = h + rms_norm(ffn, g_ffn_post[i])
        e = rms_norm(p[i] @ w_ple_proj[i], g_ple[i])
        h = h + jax.nn.sigmoid(h @ w_ple_gate[i]) * e
    return h


DEPTH_2 = 2

N_A_LAYERS = DEPTH_2 // 2
N_B_LAYERS = DEPTH_2 - N_A_LAYERS
N_HEADS = 16
HEAD_DIM = 64
N_KV_GROUPS = 4
HEADS_PER_GROUP = N_HEADS // N_KV_GROUPS
D_FF_2 = 4 * D_MODEL
CONV_WIDTH_2 = 3
CMP_BLOCK = 32
CMP_STRIDE = 16
SEL_BLOCK = 64
SEL_TOP_N = 16
WINDOW = 512
PHI_HIDDEN = 256
N_BUCKETS = 32
MAX_DISTANCE = 128
EPS = 1e-6
NEG_INF = -1e30
FORCED_SCORE = 1e9


def rms_norm_2(x, g):
    xf = x.astype(jnp.float32)
    y = xf * lax.rsqrt(jnp.mean(xf * xf, axis=-1, keepdims=True) + EPS)
    return (y * g.astype(jnp.float32)).astype(x.dtype)

def t5_bucket(dist):
    dist = jnp.maximum(dist, 0)
    max_exact = N_BUCKETS // 2
    logd = jnp.log(jnp.maximum(dist, 1).astype(jnp.float32) / max_exact)
    large = max_exact + (logd / math.log(MAX_DISTANCE / max_exact)
                         * (N_BUCKETS - max_exact)).astype(jnp.int32)
    large = jnp.minimum(large, N_BUCKETS - 1)
    return jnp.where(dist < max_exact, dist, large)

def short_conv_mixer(h, w_in, conv_w, w_out):
    S = h.shape[1]
    b_gate, c_gate, u = jnp.split(h @ w_in, 3, axis=-1)
    v = c_gate * u
    vp = jnp.pad(v, ((0, 0), (CONV_WIDTH_2 - 1, 0), (0, 0)))
    conv = sum(conv_w[k] * vp[:, k:k + S] for k in range(CONV_WIDTH_2))
    return (b_gate * conv) @ w_out

def squared_relu_mlp(h, w1, w2):
    return jnp.square(jax.nn.relu(h @ w1)) @ w2

def compress_blocks(t, pe, w1, w2):
    B, S, G, dh = t.shape
    chunks = t.reshape(B, S // CMP_STRIDE, CMP_STRIDE, G, dh)
    blocks = jnp.concatenate([chunks[:, :-1], chunks[:, 1:]], axis=2)
    blocks = blocks + pe[None, None, :, None, :]
    n_cmp = blocks.shape[1]
    flat = jnp.moveaxis(blocks, 2, 3).reshape(B, n_cmp, G, CMP_BLOCK * dh)
    return jax.nn.silu(flat @ w1) @ w2

def nsa_shared_kv(h, w_kv, cmp_pe_k, cmp_pe_v, phi_k_w1, phi_k_w2, phi_v_w1, phi_v_w2):
    B, S, _ = h.shape
    kv = (h @ w_kv).reshape(B, S, 6, N_KV_GROUPS, HEAD_DIM)
    k_raw, v_raw = kv[:, :, 0], kv[:, :, 1]
    k_sel, v_sel = kv[:, :, 2], kv[:, :, 3]
    k_win, v_win = kv[:, :, 4], kv[:, :, 5]
    k_cmp = compress_blocks(k_raw, cmp_pe_k, phi_k_w1, phi_k_w2)
    v_cmp = compress_blocks(v_raw, cmp_pe_v, phi_v_w1, phi_v_w2)
    return (k_cmp, v_cmp, k_sel, v_sel, k_win, v_win)

def nsa_attention(q, gates, k_cmp, v_cmp, k_sel, v_sel, k_win, v_win, rel_bias):
    B, S, G, Hg, dh = q.shape
    n_cmp = k_cmp.shape[1]
    n_selb = S // SEL_BLOCK
    top_n = min(SEL_TOP_N, n_selb)
    n_qb = S // Q_BLOCK
    bias_g = rel_bias.reshape(N_BUCKETS, G, Hg)

    cmp_end = jnp.arange(n_cmp) * CMP_STRIDE + CMP_BLOCK - 1
    ratio = SEL_BLOCK // CMP_STRIDE
    span = CMP_BLOCK // CMP_STRIDE
    offs = (jnp.arange(ratio)[:, None] - jnp.arange(span)[None, :]).reshape(-1)
    map_idx = ratio * jnp.arange(n_selb)[:, None] + offs[None, :]
    map_ok = (map_idx >= 0) & (map_idx < n_cmp)
    map_idx = jnp.clip(map_idx, 0, n_cmp - 1)

    k_sel_bg = jnp.transpose(k_sel.reshape(B, n_selb, SEL_BLOCK, G, dh), (0, 3, 1, 2, 4))
    v_sel_bg = jnp.transpose(v_sel.reshape(B, n_selb, SEL_BLOCK, G, dh), (0, 3, 1, 2, 4))
    k_win_p = jnp.pad(k_win, ((0, 0), (WINDOW, 0), (0, 0), (0, 0)))
    v_win_p = jnp.pad(v_win, ((0, 0), (WINDOW, 0), (0, 0), (0, 0)))
    b_ix = jnp.arange(B)[:, None, None, None]
    g_ix = jnp.arange(G)[None, None, :, None]
    jb = jnp.arange(n_selb)

    def one_block(qb):
        t0 = qb * Q_BLOCK
        qt = lax.dynamic_slice_in_dim(q, t0, Q_BLOCK, axis=1)
        gt = lax.dynamic_slice_in_dim(gates, t0, Q_BLOCK, axis=1)
        pos = t0 + jnp.arange(Q_BLOCK)

        d_c = pos[:, None] - cmp_end[None, :]
        valid_c = d_c >= 0
        bias_c = jnp.transpose(bias_g[t5_bucket(d_c)], (0, 2, 3, 1)).astype(jnp.float32)
        logit_c = jnp.einsum('bqghd,bngd->bqghn', qt, k_cmp).astype(jnp.float32) + bias_c[None]
        logit_c = jnp.where(valid_c[None, :, None, None, :], logit_c, NEG_INF)
        has_any = jnp.any(valid_c, axis=-1).astype(jnp.float32)
        p_c = jax.nn.softmax(logit_c, axis=-1) * has_any[None, :, None, None, None]
        o_c = jnp.einsum('bqghn,bngd->bqghd', p_c.astype(v_cmp.dtype), v_cmp)

        imp = p_c.sum(axis=3)
        imp_s = jnp.sum(jnp.where(map_ok, jnp.take(imp, map_idx, axis=-1), 0.0), axis=-1)
        cb = pos // SEL_BLOCK
        forced = (jb[None, :] == 0) | (jb[None, :] == cb[:, None]) | (jb[None, :] == cb[:, None] - 1)
        future = jb[None, :] > cb[:, None]
        score = jnp.where(forced[None, :, None, :], FORCED_SCORE, imp_s)
        score = jnp.where(future[None, :, None, :], NEG_INF, score)
        top_s, top_idx = lax.top_k(score, top_n)
        blk_ok = top_s > NEG_INF * 0.5

        ks = k_sel_bg[b_ix, g_ix, top_idx].reshape(B, Q_BLOCK, G, top_n * SEL_BLOCK, dh)
        vs = v_sel_bg[b_ix, g_ix, top_idx].reshape(B, Q_BLOCK, G, top_n * SEL_BLOCK, dh)
        kpos = (top_idx[..., None] * SEL_BLOCK + jnp.arange(SEL_BLOCK)).reshape(B, Q_BLOCK, G, -1)
        blk_ok_k = jnp.repeat(blk_ok, SEL_BLOCK, axis=-1)
        d_s = pos[None, :, None, None] - kpos
        valid_s = blk_ok_k & (d_s >= 0)
        bias_s = jnp.transpose(bias_g[t5_bucket(d_s), g_ix], (0, 1, 2, 4, 3)).astype(jnp.float32)
        logit_s = jnp.einsum('bqghd,bqgkd->bqghk', qt, ks).astype(jnp.float32) + bias_s
        logit_s = jnp.where(valid_s[:, :, :, None, :], logit_s, NEG_INF)
        p_s = jax.nn.softmax(logit_s, axis=-1)
        o_s = jnp.einsum('bqghk,bqgkd->bqghd', p_s.astype(vs.dtype), vs)

        kw = lax.dynamic_slice_in_dim(k_win_p, t0, Q_BLOCK + WINDOW, axis=1)
        vw = lax.dynamic_slice_in_dim(v_win_p, t0, Q_BLOCK + WINDOW, axis=1)
        wpos = t0 - WINDOW + jnp.arange(Q_BLOCK + WINDOW)
        d_w = pos[:, None] - wpos[None, :]
        valid_w = (d_w >= 0) & (d_w < WINDOW) & (wpos[None, :] >= 0)
        bias_w = jnp.transpose(bias_g[t5_bucket(d_w)], (0, 2, 3, 1)).astype(jnp.float32)
        logit_w = jnp.einsum('bqghd,bkgd->bqghk', qt, kw).astype(jnp.float32) + bias_w[None]
        logit_w = jnp.where(valid_w[None, :, None, None, :], logit_w, NEG_INF)
        p_w = jax.nn.softmax(logit_w, axis=-1)
        o_w = jnp.einsum('bqghk,bkgd->bqghd', p_w.astype(vw.dtype), vw)

        o = gt[..., 0:1] * o_c + gt[..., 1:2] * o_s + gt[..., 2:3] * o_w
        return o.astype(q.dtype)

    o = lax.map(one_block, jnp.arange(n_qb))
    return jnp.moveaxis(o, 0, 1).reshape(B, S, G, Hg, dh)

def nsa_mixer(h, w_qg, w_o, shared, rel_bias):
    B, S, _ = h.shape
    qg = h @ w_qg
    q = qg[..., :N_HEADS * HEAD_DIM].reshape(B, S, N_KV_GROUPS, HEADS_PER_GROUP, HEAD_DIM)
    q = q * (HEAD_DIM ** -0.5)
    gates = jax.nn.sigmoid(qg[..., N_HEADS * HEAD_DIM:].astype(jnp.float32))
    gates = gates.reshape(B, S, N_KV_GROUPS, HEADS_PER_GROUP, 3)
    k_cmp, v_cmp, k_sel, v_sel, k_win, v_win = shared
    o = nsa_attention(q, gates, k_cmp, v_cmp, k_sel, v_sel, k_win, v_win, rel_bias)
    return o.reshape(B, S, N_HEADS * HEAD_DIM) @ w_o

def second_inputs(seed: int = 0) -> dict:
    key = jax.random.key(seed)
    ks = jax.random.split(key, 22)
    f32 = jnp.float32
    D, H, G, dh = D_MODEL, N_HEADS, N_KV_GROUPS, HEAD_DIM

    def nrm(k, shape, scale):
        return jax.random.normal(k, shape, f32) * scale

    return {
        "x": nrm(ks[0], (BATCH, SEQ, D), 1.0),
        "rel_bias": nrm(ks[1], (N_BUCKETS, H), 0.5),
        "norm_mix": 1.0 + nrm(ks[2], (DEPTH_2, D), 0.1),
        "norm_mlp": 1.0 + nrm(ks[3], (DEPTH_2, D), 0.1),
        "mlp_w1": nrm(ks[4], (DEPTH_2, D, D_FF_2), D ** -0.5),
        "mlp_w2": nrm(ks[5], (DEPTH_2, D_FF_2, D), 0.5 * D_FF_2 ** -0.5),
        "a_w_in": nrm(ks[6], (N_A_LAYERS, D, 3 * D), D ** -0.5),
        "a_conv_w": nrm(ks[7], (N_A_LAYERS, CONV_WIDTH_2, D), CONV_WIDTH_2 ** -0.5),
        "a_w_out": nrm(ks[8], (N_A_LAYERS, D, D), D ** -0.5),
        "kv_norm": 1.0 + nrm(ks[9], (D,), 0.1),
        "w_kv": nrm(ks[10], (D, 6 * G * dh), D ** -0.5),
        "cmp_pe_k": nrm(ks[11], (CMP_BLOCK, dh), 0.1),
        "cmp_pe_v": nrm(ks[12], (CMP_BLOCK, dh), 0.1),
        "phi_k_w1": nrm(ks[13], (CMP_BLOCK * dh, PHI_HIDDEN), (CMP_BLOCK * dh) ** -0.5),
        "phi_k_w2": nrm(ks[14], (PHI_HIDDEN, dh), PHI_HIDDEN ** -0.5),
        "phi_v_w1": nrm(ks[15], (CMP_BLOCK * dh, PHI_HIDDEN), (CMP_BLOCK * dh) ** -0.5),
        "phi_v_w2": nrm(ks[16], (PHI_HIDDEN, dh), PHI_HIDDEN ** -0.5),
        "b_w_qg": nrm(ks[17], (N_B_LAYERS, D, H * dh + 3 * H), D ** -0.5),
        "b_w_o": nrm(ks[18], (N_B_LAYERS, H * dh, D), (H * dh) ** -0.5),
        "final_norm": 1.0 + nrm(ks[19], (D,), 0.1),
    }

def second_block(x, rel_bias, norm_mix, norm_mlp, mlp_w1, mlp_w2, a_w_in, a_conv_w, a_w_out,
              kv_norm, w_kv, cmp_pe_k, cmp_pe_v, phi_k_w1, phi_k_w2, phi_v_w1, phi_v_w2,
              b_w_qg, b_w_o, final_norm):
    shared = None
    for layer in range(DEPTH_2):
        h = rms_norm_2(x, norm_mix[layer])
        if layer < N_A_LAYERS:
            x = x + short_conv_mixer(h, a_w_in[layer], a_conv_w[layer], a_w_out[layer])
        else:
            i = layer - N_A_LAYERS
            x = x + nsa_mixer(h, b_w_qg[i], b_w_o[i], shared, rel_bias)
        x = x + squared_relu_mlp(rms_norm_2(x, norm_mlp[layer]), mlp_w1[layer], mlp_w2[layer])
        if layer == N_A_LAYERS - 1:
            shared = nsa_shared_kv(rms_norm_2(x, kv_norm), w_kv, cmp_pe_k, cmp_pe_v,
                                   phi_k_w1, phi_k_w2, phi_v_w1, phi_v_w2)
    return rms_norm_2(x, final_norm)


def setup_inputs(seed=0):
    out = dict(first_inputs(seed))
    for name, value in second_inputs(seed + 1).items():
        if name != "x":
            out[name + "_2"] = value
    return out


def reference(
    x, p, positions, g_mix_pre, w_in, g_q_a, w_q_b, g_kv_a, w_kv_b, conv_w, conv_b, conv_ln_g,
    conv_ln_b, w_o, g_mix_post, g_ffn_pre, w_ffn_gate, w_ffn_up, ffn_dw_w, ffn_dw_b, w_ffn_down,
    g_ffn_post, w_ple_proj, g_ple, w_ple_gate, rel_bias_2, norm_mix_2, norm_mlp_2, mlp_w1_2,
    mlp_w2_2, a_w_in_2, a_conv_w_2, a_w_out_2, kv_norm_2, w_kv_2, cmp_pe_k_2, cmp_pe_v_2,
    phi_k_w1_2, phi_k_w2_2, phi_v_w1_2, phi_v_w2_2, b_w_qg_2, b_w_o_2, final_norm_2,
):
    x = first_block(
        x, p, positions, g_mix_pre, w_in, g_q_a, w_q_b, g_kv_a, w_kv_b, conv_w, conv_b,
        conv_ln_g, conv_ln_b, w_o, g_mix_post, g_ffn_pre, w_ffn_gate, w_ffn_up, ffn_dw_w,
        ffn_dw_b, w_ffn_down, g_ffn_post, w_ple_proj, g_ple, w_ple_gate,
    )
    return second_block(
        x, rel_bias_2, norm_mix_2, norm_mlp_2, mlp_w1_2, mlp_w2_2, a_w_in_2, a_conv_w_2,
        a_w_out_2, kv_norm_2, w_kv_2, cmp_pe_k_2, cmp_pe_v_2, phi_k_w1_2, phi_k_w2_2,
        phi_v_w1_2, phi_v_w2_2, b_w_qg_2, b_w_o_2, final_norm_2,
    )


_drawn_inputs = setup_inputs


def setup_inputs(seed=0):
    import zlib

    import numpy as np

    out = dict(_drawn_inputs(seed))
    spreads = {}
    factors = {'g_q_a': 4.992,
     'g_kv_a': 3.269,
     'conv_b': 8.456,
     'conv_ln_b': 18.153,
     'ffn_dw_b': 8.0,
     'g_ple': 2.901,
     'kv_norm_2': 4.213,
     'cmp_pe_k_2': 8.0,
     'cmp_pe_v_2': 4.277,
     'conv_ln_g': 2.925}
    for name, (base, spread) in spreads.items():
        noise = np.random.default_rng([zlib.crc32(name.encode()), seed]).standard_normal(out[name].shape)
        drawn = base * np.exp(spread * noise) if base else spread * noise
        out[name] = __import__('jax').numpy.asarray(drawn.astype(out[name].dtype))
    for name, factor in factors.items():
        out[name] = (out[name] * factor).astype(out[name].dtype)
    return out
```

```python
import math
from contextlib import ExitStack

import numpy as np
import concourse.bass as bass
from concourse import mybir

S, D, P = 512, 1024, 128
DC, TT = D // P, S // P
H1, NOPE, ROPE, VD = 8, 64, 32, 64
QR, KVR = 384, 256
CC, CW = 512, 31
FF, FC = 2816, 22
H2, GR, HD = 16, 4, 64
HG = H2 // GR
NCMP = 31
FF2C = 32
PHI = 256
EPS = 1e-6
NEG = -1e30
NSLOT = 4
SC1 = float(NOPE + ROPE) ** -0.5
SC2 = float(HD) ** -0.5

VECS = [("g_mix_pre", 8), ("g_q_a", 3), ("g_kv_a", 2), ("conv_b", 4), ("conv_ln_g", 4), ("conv_ln_b", 4),
        ("g_mix_post", 8), ("g_ffn_pre", 8), ("ffn_dw_b", 22), ("g_ffn_post", 8), ("g_ple", 8),
        ("norm_mix_0", 8), ("norm_mix_1", 8), ("norm_mlp_0", 8), ("norm_mlp_1", 8), ("kv_norm", 8),
        ("final_norm", 8), ("conv_w", CW * 4), ("ffn_dw_w", 3 * FC), ("a_conv_w", 3 * DC),
        ("freq", 1), ("cosine", 1), ("quarter", 1), ("sign", 1), ("has_any", 1), ("pe_k", 16), ("pe_v", 16)]
VO, NV = {}, 0
for _name, _n in VECS:
    VO[_name] = NV
    NV += _n

UNITS = [("in_proj", 14), ("q_b", 4), ("kv_b", 2), ("o", 8), ("ple", 2), ("ffn", 66), ("ple_gate", 8),
         ("a_in", 24), ("a_out", 8), ("mlp0", 64), ("kv", 12), ("phi", 8), ("q2", 8), ("gates", 1),
         ("o2", 8), ("mlp1", 64)]
NU = sum(n for _, n in UNITS)

UO, _at = {}, 0
for _name, _n in UNITS:
    UO[_name] = _at
    _at += _n
TURN = (6.28125, float(np.float32(0.0019350051879882812)), float(np.float32(2 * math.pi - 6.28125 - 0.0019350051879882812)))


SEMS = """whi wlo used tile_done tile_free x_hi x_lo sq_done acc_add norm_sum norm_std norm_inv h_upd
 mask_in ident_in vec_in rope_in x_in p_in onehot_in relb_in w2_in const_ok ang ang_k ang_kf ang_r0 ang_r1 ang_r2 rope_sin
 gt_sig c_ok qkv_g qkv_hi qkv_lo kr_part kr_rope kr_copy qt_nope qt_r qt_rope q_hi q_lo k_half
 k_hi k_lo taps conv_mean conv_xc conv_xn conv_act
 s_done l_done neg_max p_exp p_inv p_norm t_done pt_act pt_dve o_done o_out
 y_out y_tmp e_out e_g pconv ffn_t ffn_g ffn_gelu ffn_u hid_s hid_hi hid_lo
 r_ok v_ok y_ok cu_t tab_done tab_out tab_st strip_in bc_in col_done col_ok kv_ok
 kr_ok kr_pad kr_hi kr_lo bias_ok silu_ok cmp_done kc_hi kc_lo vc_ok gate_s gate_ok
 c_lg c_mx c_sub c_exp c_sum c_inv c_mul c_tr c_pt krep krep_hi krep_lo o_hi ple_s ple_m out_ok out_st""".split()


class Mark:

    def __init__(self, sem, state):
        self.sem, self.state, self.n, self.step = sem, state, 0, 0

    def upto(self, k=0):
        v = self.n + k
        return (self.sem, v + self.step * self.state.i) if self.step else (self.sem, v)

    def tick(self):
        self.n += 1
        return self.sem, 1

    def next(self, k=1):
        self.n += k
        return self.upto()


class Turn:

    def __init__(self):
        self.i = 0


class Job:

    def __init__(self, qh, ql, kh, kl, v, p, pt, out, bias, scale, gate):
        self.qh, self.ql, self.kh, self.kl, self.v, self.p, self.pt = qh, ql, kh, kl, v, p, pt
        self.out, self.bias, self.scale, self.gate = out, bias, scale, gate


class Book:

    def __init__(self, sems):
        self.state = Turn()
        self.m = {k: Mark(v, self.state) for k, v in sems.items()}
        self.u = self.du = 0
        self.t = 0
        self.ahead = 0

    def turns(self, eng, count, du, steps):
        return _turns(self, eng, count, du, steps)


def _turns(book, eng, count, du, steps):
    from contextlib import contextmanager

    @contextmanager
    def run():
        n0 = {k: v.n for k, v in book.m.items()}
        u0, t0, a0 = book.u, book.t, book.ahead
        for k, v in steps.items():
            book.m[k].step = v
        book.du = du
        with eng.Fori(0, count) as i:
            book.state.i = i
            yield i
        book.state.i, book.du = 0, 0
        for k, v in book.m.items():
            got = v.n - n0[k]
            assert got == steps.get(k, 0), (k, got, steps.get(k, 0))
            v.n, v.step = n0[k] + got * count, 0
        assert book.u - u0 == du and book.ahead - a0 in (0, du) and (book.t - t0) % 4 == 0
        book.t = t0 + (book.t - t0) * count
        book.u = u0 + du * count
        book.ahead = a0 + (book.ahead - a0) * count
    return run()


def build(nc, io):
    f32, f32r = mybir.dt.float32, mybir.dt.float32r
    ACT, ALU, AX = mybir.ActivationFunctionType, mybir.AluOpType, mybir.AxisListType
    MUL, ADD, SUB, MAX = ALU.mult, ALU.add, ALU.subtract, ALU.max
    with ExitStack() as ctx:
        def sb(name, shape, dt=f32):
            return ctx.enter_context(nc.sbuf_tensor(name, shape, dt))

        raw = sb("raw", [P, NSLOT, 1024])
        WH = sb("WH", [P, NSLOT, 1024], f32r)
        WL = sb("WL", [P, NSLOT, 1024], f32r)
        XH = sb("XH", [P, DC, S], f32r)
        XL = sb("XL", [P, DC, S], f32r)
        HH = sb("HH", [P, DC, S], f32r)
        HL = sb("HL", [P, DC, S], f32r)
        h = sb("h", [P, DC, S])
        rstd = sb("rstd", [P, S])
        acc = sb("acc", [P, S])
        sq = sb("sq", [P, 2, S])
        vec = sb("vec", [P, NV])
        ident = sb("ident", [P, P])
        ones = sb("ones", [P, P])
        small = sb("small", [P, 256])
        ARENA = 16384
        ar = sb("arena", [P, ARENA])
        ps = ctx.enter_context(nc.psum_tensor("ps", [P, 8, S], f32))
        place = [0]

        def cut(n, at=None):
            if at is not None:
                place[0] = at
            a = place[0]
            place[0] += n
            assert place[0] <= ARENA, (place[0], ARENA)
            return ar[:, a:a + n]

        def cut(start, *shape):
            n = int(np.prod(shape))
            assert start + n <= ARENA, (start, n)
            v = ar[:, start:start + n]
            return v.rearrange("p (a b) -> p a b", a=shape[0]) if len(shape) == 2 else v

        PADW = S + CW - 1
        cpad = cut(0, 4, PADW)
        cacc = cut(2168, 4, S)
        V1 = cut(4216, TT, S)
        khat = cut(6264, H1, S)
        O1 = cut(6264, 4, S)
        mask1 = cut(10360, S)
        qkv = cut(10872, 5, S)
        gt = cut(13432, 2, S)
        rope = cut(14456, S)
        qt = cut(14968, 2, S)
        PB1 = [cut(x, 1280) for x in (10872, 12152, 8312)]
        PT1 = cut(13432, 2, 1280)
        Y = cut(0, DC, S)
        ple = cut(4096, DC, S)
        gpad = cut(8192, 2, S + 2)
        gc_ = cut(9232, 2, S)
        up = cut(10256, 2, S)
        ftmp = cut(11280, 2, S)
        ptmp = cut(12304, 2, S)
        xp = cut(13328, 2, S)

        rr, acs, apad = cut(0, S), cut(512, 2, S), cut(1536, 2, S + 2)
        act_, abs_, ay = cut(2564, 2, S), cut(3588, 2, S), cut(4612, 2, S)
        ohs, relb, tabs, bcs = cut(12304, 1680), cut(13984, 2 * H2), cut(5636, 640), cut(9728, TT, S)
        rt, st_ = cut(0, 4, S), cut(2048, 4, S)
        K32, V2 = cut(0, 2 * GR, S), cut(4096, TT, S)
        KR = [cut(6600 + 1320 * i, 5, 264) for i in range(2)]
        FH = [XH[:, :, :].rearrange("p a b -> p (a b)")[:, 1320 * i:1320 * i + 1320].rearrange("p (g n) -> p g n", g=5)
              for i in range(2)]
        FL = [XL[:, :, :].rearrange("p a b -> p (a b)")[:, 1320 * i:1320 * i + 1320].rearrange("p (g n) -> p g n", g=5)
              for i in range(2)]
        w2s, hid, VC, GT, pre = cut(14848, 384), cut(15232, 4, P), cut(16128, HD), cut(16192, TT, 48), cut(15744, 2, 160)
        qst, L, PCT = cut(6144, TT, S), cut(12288, TT, S), cut(6144, HG, S)
        strips, PB2, PT2, O2 = cut(8192, 3, S), cut(9728, 3, 1280), cut(13568, 2, 1280), cut(0, DC, S)

        NMX, SUM, INV, MXC = 16, 32, 48, 64
        POFF = (0, 128, 384, 768)
        SCORES = ((0, 0, 0), (1, 0, P), (2, 1, 0), (3, 2, 0))
        TRANSPOSES = (tuple((0, q, q * P) for q in range(4)),
                      tuple((1, q, (q - 1) * P) for q in range(1, 4)) + ((3, 3, 3 * P),),
                      tuple((2, q, (q - 2) * P) for q in range(2, 4)))
        TBANK = (4, 5, 7)
        VALUES = (((0, 0),), ((1, 512), (3, 896)), ((2, 1024),))

        def LAST_OF_BANK(n, bk):
            k, g = divmod(3 * n + bk - 4, 3)
            return 4 * k + g + 2

        def job1(n):
            pair, r = divmod(n, 2)
            return Job(
                qh=XH[0:96, n, :], ql=XL[0:96, n, :], kh=HH[0:96, n, :], kl=HL[0:96, n, :],
                v=lambda kt: V1[:, kt, n * VD:(n + 1) * VD], p=lambda k: PB1[k % 3], pt=lambda k: PT1[:, k % 2, :],
                out=ps[64 * r:64 * r + 64, 6, :], bias=mask1, scale=SC1, gate=None)

        def job2(n):
            hd, br = divmod(n, 2)
            pair, r = divmod(hd, 2)
            g = hd // HG
            x = slice(64 * r, 64 * r + 64)
            return Job(
                qh=XH[x, pair, :], ql=XL[x, pair, :], kh=HH[x, br * GR + g, :], kl=HL[x, br * GR + g, :],
                v=lambda kt: V2[:, kt, br * 256 + HD * g:br * 256 + HD * g + HD], p=lambda k: PB2[:, k % 3, :],
                pt=lambda k: PT2[:, k % 2, :], out=ps[x, 6, :], bias=strips[:, hd % 3, :], scale=1.0,
                gate=GT[:, :, 3 * hd + 1 + br])

        JOBS2 = [job2(n) for n in range(2 * H2)]
        JOBS1 = [job1(n) for n in range(H1)]

        strip_in = [ctx.enter_context(nc.semaphore(f"strip_in{s}")) for s in range(3)]
        KCH = sb("KCH", [P, P], f32r)
        KCL = sb("KCL", [P, P], f32r)

        sems = {name: ctx.enter_context(nc.semaphore(name)) for name in SEMS}
        raw_in = [ctx.enter_context(nc.semaphore(f"raw_in{s}")) for s in range(NSLOT)]

        def col(name, c=0):
            return vec[:, VO[name] + c:VO[name] + c + 1]

        def raw_ready(b, k):
            u = b.u + k if not isinstance(k, tuple) else k[0]
            return raw_in[u % NSLOT], 16 * (u // NSLOT + 1) + (16 * (b.du // NSLOT) * b.state.i if b.du else 0)

        def units(b, n, k=0):
            return n + k + (b.du * b.state.i if b.du else 0)

        block = ctx.enter_context(nc.Block())

        @block.sync
        def _(sp):
            sp.dma_start(h[:, :, :], io["xT"].rearrange("(c p) n -> p c n", p=P)).then_inc(sems["x_in"], 16)
            for u in range(NSLOT):
                sp.dma_start(raw[:, u, :], io["weights"][u]).then_inc(raw_in[u], 16)

            def weights(a, b):
                full = (b - a) // NSLOT
                if full:
                    with sp.Fori(0, full) as i:
                        for k in range(NSLOT):
                            sp.wait_ge(sems["wlo"], NSLOT * i + a + k - NSLOT + 1)
                            sp.dma_start(raw[:, (a + k) % NSLOT, :], io["weights"][NSLOT * i + (a + k)])\
                              .then_inc(raw_in[(a + k) % NSLOT], 16)
                for u in range(a + full * NSLOT, b):
                    sp.wait_ge(sems["wlo"], u - NSLOT + 1)
                    sp.dma_start(raw[:, u % NSLOT, :], io["weights"][u]).then_inc(raw_in[u % NSLOT], 16)

            weights(NSLOT, UO["o2"] + NSLOT)
            sp.wait_ge(sems["tab_st"], 16)
            for hd in range(H2):
                if hd < 3:
                    sp.wait_ge(sems["kr_lo"], 2)
                else:
                    sp.wait_ge(sems["l_done"], 4 * H1 + 8 * (hd - 2))
                sp.dma_start(strips[:, hd % 3, :], bass.AP(io["tab"].tensor, hd * 640 * P + 127, [[639, P], [1, S]]))\
                  .then_inc(strip_in[hd % 3], 16)
            weights(UO["o2"] + NSLOT, NU)
            for c in range(DC):
                sp.wait_ge(sems["out_ok"], c + 1)
                sp.dma_start(io["out"][c * P:(c + 1) * P, :], h[:, c, :]).then_inc(sems["out_st"], 16)
            sp.wait_ge(sems["out_st"], 16 * DC)

        @block.gpsimd
        def _(pool):
            nc.gpsimd.memset(ones[:, :], 1.0).then_inc(sems["const_ok"], 1)
            nc.gpsimd.memset(cpad[:, :, 0:CW - 1], 0.0).then_inc(sems["const_ok"], 1)

            def lower(u, s):
                pool.wait_ge(sems["whi"], u + 1)
                nc.gpsimd.tensor_tensor(WL[:, s, :], raw[:, s, :], WH[:, s, :].bitcast(f32), SUB)\
                  .then_inc(sems["wlo"], 1)

            with pool.Fori(0, NU // NSLOT) as i:
                for k in range(NSLOT):
                    lower(NSLOT * i + k, k)
            for u in range(NU // NSLOT * NSLOT, NU):
                lower(u, u % NSLOT)

        @block.tensor
        def _(pe):
            b = Book(sems)
            m = b.m

            def three(out, wh, wl, xh, xl, start, stop):
                nc.tensor.matmul(out, wh, xh, start=start, stop=False)
                nc.tensor.matmul(out, wh, xl, start=False, stop=False)
                return nc.tensor.matmul(out, wl, xh, start=False, stop=stop)

            def project(nu, nk, nt, xh, xl, x_sem=None, cols=lambda x, c: x[:, c, :], n=S):
                for j in range(nu):
                    pe.wait_ge(sems["wlo"], units(b, b.u, j + 1))
                    s = (b.u + j) % NSLOT
                    for t in range(nt):
                        if j == 0 and b.t + t >= 4:
                            pe.wait_ge(*m["tile_free"].upto(t - 3))
                        for k in range(nk):
                            c = j * nk + k
                            if t == 0 and x_sem is not None:
                                pe.wait_ge(*x_sem.upto(c + 1))
                            w = slice(k * nt * P + t * P, k * nt * P + (t + 1) * P)
                            last = three(ps[:, (b.t + t) % 4, 0:n], WH[:, s, w], WL[:, s, w], cols(xh, c), cols(xl, c),
                                         c == 0, c == nu * nk - 1)
                        if t == nt - 1:
                            last.then_inc(*m["used"].tick())
                        elif j == nu - 1:
                            last.then_inc(*m["tile_done"].tick())
                b.u += nu
                b.t += nt
                m["tile_free"].n += nt

            def by_token(nu, nk, n, xh, xl):
                for j in range(nu):
                    pe.wait_ge(sems["wlo"], units(b, b.u, j + 1))
                    s = (b.u + j) % NSLOT
                    for t in range(TT):
                        if j == 0:
                            pe.wait_ge(*m["tile_free"].upto(t - 3))
                        for k in range(nk):
                            c = j * nk + k
                            x = slice(t * P, (t + 1) * P)
                            last = three(ps[:, (b.t + t) % 4, 0:n], xh[:, c, x], xl[:, c, x],
                                         WH[:, s, k * n:(k + 1) * n], WL[:, s, k * n:(k + 1) * n],
                                         c == 0, c == nu * nk - 1)
                        if t == TT - 1:
                            last.then_inc(*m["used"].tick())
                        elif j == nu - 1:
                            last.then_inc(*m["tile_done"].tick())
                b.u += nu
                b.t += TT
                m["tile_free"].n += TT

            def total(n, bank=7):
                pe.wait_ge(*m["acc_add"].next(n))
                nc.tensor.matmul(ps[:, bank, :], ones[:, :], acc[:, :], start=True, stop=True)\
                  .then_inc(*m["norm_sum"].tick())

            def scores(n, job):
                for qs, bk, at in SCORES:
                    bank = (3 * n + bk) % 4
                    if at == 0:
                        if (3 * n + bk) >= 4:
                            pe.wait_ge(*m["l_done"].upto(LAST_OF_BANK(n, bk)))
                        else:
                            pe.wait_ge(*m["tile_free"].upto())
                    w = P * (qs + 1)
                    q = slice(qs * P, w)
                    last = three(ps[:, bank, at:at + w], job.qh[:, q], job.ql[:, q], job.kh[:, 0:w], job.kl[:, 0:w],
                                 True, True)
                    if qs:
                        last.then_inc(*m["s_done"].tick())

            def transposes(n, job):
                m["p_norm"].next(4)
                pe.wait_ge(*m["p_norm"].upto())
                for g, group in enumerate(TRANSPOSES):
                    c = 3 * n + g
                    if c >= 3:
                        pe.wait_ge(*m["pt_act"].upto(c - 2))
                    for kt, qs, at in group:
                        last = nc.tensor.transpose(ps[:, TBANK[g], at:at + P],
                                                   job.p(n)[:, POFF[qs] + kt * P:POFF[qs] + (kt + 1) * P], ident[:, :])
                    last.then_inc(*m["t_done"].tick())

            def values(n, job, first, last):
                for g, kts in enumerate(VALUES):
                    pe.wait_ge(*m["pt_act"].upto(3 * n + g + 1))
                    for kt, at in kts:
                        done = nc.tensor.matmul(job.out[:, kt * P:S], job.v(kt), job.pt(n)[:, at:at + S - kt * P],
                                                start=first and kt == 0, stop=last and (g, kt) == (2, 2),
                                                skip_group_check=True)
                done.then_inc(*m["o_done"].tick())

            def tables():
                pe.wait_ge(sems["onehot_in"], 16)
                pe.wait_ge(sems["relb_in"], 16)
                for k, w in ((0, 512), (1, 128)):
                    nc.tensor.matmul(ps[0:H2, 4 + k, 0:w], relb[0:33, 0:H2], ohs[0:33, 512 * k:512 * k + w],
                                     start=True, stop=True).then_inc(*m["tab_done"].tick())
                for t in range(TT):
                    pe.wait_ge(*m["tab_out"].upto(t + 1))
                    for n in range(32):
                        at = 640 + P * t - 16 * n + 496
                        last = nc.tensor.matmul(ps[:, 4 + t % 2, n:S:32], ohs[0:33, at:at + P], relb[0:33, H2:2 * H2],
                                                start=True, stop=True)
                    last.then_inc(*m["tab_done"].tick())
                m["tab_out"].next(6)

            pe.wait_ge(sems["const_ok"], 2)

            pe.wait_ge(sems["vec_in"], 16)
            project(2, 4, 2, XH, XL, m["x_lo"])
            total(7)
            m["x_lo"].next(DC)
            for _ in range(4):
                project(2, 4, 2, XH, XL)
            total(2)
            for _ in range(2):
                project(2, 4, 2, XH, XL)
            total(1)
            for j in range(4):
                project(1, 3, 2, HH, HL, m["qkv_lo"] if j == 0 else None)
            m["qkv_lo"].next(3)
            project(1, 2, 4, HH[:, 3:5, :], HL[:, 3:5, :], m["qkv_lo"])
            m["qkv_lo"].next(2)
            by_token(1, 2, S, HH[:, 3:5, :], HL[:, 3:5, :])

            pe.wait_ge(sems["ident_in"], 16)
            for n in range(H1 + 3):
                if n < H1:
                    pe.wait_ge(*m["q_lo"].upto(n + 1))
                    pe.wait_ge(*m["k_lo"].upto(n + 1))
                    scores(n, JOBS1[n])
                if n >= 3:
                    k = n - 3
                    if k % 2 == 0 and k >= 2:
                        pe.wait_ge(*m["o_out"].upto(k // 2))
                    values(k, JOBS1[k], True, True)
                if 2 <= n <= H1 + 1:
                    transposes(n - 2, JOBS1[n - 2])
            m["l_done"].next(4 * H1)
            m["pt_act"].next(3 * H1)
            m["o_out"].next(H1 // 2)
            m["q_lo"].next(H1)
            m["k_lo"].next(H1)

            pe.wait_ge(*m["o_out"].upto())
            total(3)
            pe.wait_ge(*m["conv_xc"].next(4))
            total(3)
            for j in range(4):
                project(2, 4, 2, XH, XL, m["x_lo"] if j == 0 else None)
            m["x_lo"].next(DC)
            total(7)

            for j in range(2):
                project(1, 2, 4, HH, HL, m["hid_lo"] if j == 0 else None)
            m["hid_lo"].next(2)
            total(7)

            def ffn_up(pairs, x_sem=None):
                for j in range(pairs):
                    project(2, 4, 2, XH, XL, x_sem if j == 0 else None)
                    if j == 0 and x_sem is not None:
                        x_sem.next(DC)
                        total(7)
                    project(2, 4, 2, XH, XL)

            def down(par, last=False):
                pe.wait_ge(*m["hid_lo"].next(2 if last else 4))
                if last:
                    for _ in range(2):
                        project(1, 2, 4, HH[:, par * 4:par * 4 + 2, :], HL[:, par * 4:par * 4 + 2, :])
                else:
                    for _ in range(4):
                        project(1, 4, 2, HH[:, par * 4:par * 4 + 4, :], HL[:, par * 4:par * 4 + 4, :])

            ffn_up(2, m["x_lo"])
            with b.turns(pe, 2, 24, dict(used=24, tile_done=16, tile_free=32, hid_lo=8)):
                for par in range(2):
                    ffn_up(2)
                    down(par)
            ffn_up(1)
            down(0)
            down(1, True)
            total(7)

            for j in range(4):
                project(2, 4, 2, XH, XL, m["x_lo"] if j == 0 else None)
            m["x_lo"].next(DC)

            for j in range(4):
                project(2, 4, 2, HH, HL, m["x_lo"] if j == 0 else None)
                if j == 0:
                    m["x_lo"].next(DC)
                    total(7)
                project(2, 4, 2, HH, HL)
                project(2, 4, 2, HH, HL)
                if j == 1:
                    tables()
            for j in range(4):
                project(2, 4, 2, XH, XL, m["x_lo"] if j == 0 else None)
            m["x_lo"].next(DC)

            def mlp():
                def up_(par, x_sem=None):
                    project(2, 4, 2, HH, HL, x_sem)
                    if x_sem is not None:
                        x_sem.next(DC)
                        total(7)
                    project(2, 4, 2, HH, HL)

                def down_(par):
                    pe.wait_ge(*m["hid_lo"].next(4))
                    for _ in range(4):
                        project(1, 4, 2, XH[:, par * 4:par * 4 + 4, :], XL[:, par * 4:par * 4 + 4, :])

                up_(0, m["x_lo"])
                with b.turns(pe, 3, 16, dict(used=16, tile_done=12, tile_free=24, hid_lo=8)):
                    for par in range(2):
                        up_(1 - par)
                        down_(par)
                up_(1)
                down_(0)
                down_(1)

            mlp()

            for j in range(3):
                project(2, 4, 2, HH, HL, m["x_lo"] if j == 0 else None)
                if j == 0:
                    m["x_lo"].next(DC)
                    total(7)
                    project(2, 4, 2, HH, HL)
                    m["norm_inv"].n = m["norm_sum"].n - 1
                    pe.wait_ge(*m["norm_inv"].upto())
                    for t in range(TT):
                        last = nc.tensor.transpose(ps[:, 6, t * P:(t + 1) * P], rstd[:, t * P:(t + 1) * P], ident[:, :])
                    last.then_inc(*m["col_done"].tick())
                else:
                    by_token(2, 4, 256, HH, HL)
            for i in range(2):
                pe.wait_ge(*m["kr_lo"].next())
                project(4, 4, 2, FH[i], FL[i], cols=lambda x, c: x[:, :, c:c + 249:8], n=5 * 32)
            pe.wait_ge(*m["col_ok"].next())
            pe.wait_ge(sems["w2_in"], 16)
            for i in range(2):
                pe.wait_ge(*m["silu_ok"].next(2))
                for c in range(2):
                    if i == 0:
                        last = nc.tensor.matmul(ps[:, 6, 0:P], w2s[:, c * P:(c + 1) * P], hid[:, c, :],
                                                start=c == 0, stop=c == 1)
                    else:
                        last = nc.tensor.matmul(ps[:, 5, 0:HD], hid[:, 2 + c, :], w2s[:, 256 + c * HD:256 + (c + 1) * HD],
                                                start=c == 0, stop=c == 1)
                last.then_inc(*m["cmp_done"].tick())
            for j in range(4):
                project(2, 4, 2, HH, HL, m["x_lo"] if j == 0 else None)
            m["x_lo"].next(DC)
            by_token(1, 8, 3 * H2, HH, HL)

            pe.wait_ge(*m["q_lo"].next(DC))
            pe.wait_ge(*m["kc_lo"].next())
            pe.wait_ge(*m["tile_free"].upto())
            for two in range(2):
                for r in range(2):
                    for t in (2 * two, 2 * two + 1):
                        x, y = slice(t * P, (t + 1) * P), slice(64 * r, 64 * r + 64)
                        for i2 in range(2):
                            for g in range(GR):
                                c = (HG * g + 2 * i2 + r) // 2
                                at = 256 * (t % 2) + (i2 * GR + g) * 32
                                last = three(ps[:, 2 * two + r, at:at + 32], XH[y, c, x], XL[y, c, x],
                                             KCH[y, g * 32:g * 32 + 32], KCL[y, g * 32:g * 32 + 32], True, True)
                    last.then_inc(*m["c_lg"].tick())
            m["tile_free"].n += 2 * TT
            b.t = 0

            def compressed_transposes():
                for t in range(TT):
                    pe.wait_ge(*m["c_mul"].next())
                    if t >= 2:
                        pe.wait_ge(*m["c_pt"].upto(t - 1))
                    if t < 2:
                        pe.wait_ge(*m["vc_ok"].upto(1))
                    for i in range(HG):
                        last = nc.tensor.transpose(ps[:, 4 + t % 2, i * P:(i + 1) * P], L[:, t, i * P:(i + 1) * P],
                                                   ident[:, :])
                    last.then_inc(*m["c_tr"].tick())
                pe.wait_ge(*m["c_pt"].next(TT))

            NJ = 2 * H2
            for n in range(NJ + 3):
                if n < NJ:
                    if n == 0:
                        pe.wait_ge(*m["krep_lo"].next(2 * GR))
                    scores(n, JOBS2[n])
                if n == 0:
                    compressed_transposes()
                if n >= 3:
                    k = n - 3
                    if k % 4 == 0 and k >= 4:
                        pe.wait_ge(*m["o_out"].upto(k // 4))
                    if k == 0:
                        pe.wait_ge(*m["kc_lo"].upto())
                    if k % 2 == 0:
                        g, i = divmod(k // 2, HG)
                        nc.tensor.matmul(JOBS2[k].out, VC[32 * g:32 * g + 32, :], PCT[32 * g:32 * g + 32, i, :],
                                         start=True, stop=False, skip_group_check=True)
                    values(k, JOBS2[k], False, k % 2 == 1)
                if 2 <= n <= NJ + 1:
                    transposes(n - 2, JOBS2[n - 2])
            m["l_done"].next(4 * NJ)
            m["pt_act"].next(3 * NJ)
            m["o_out"].next(DC)
            for j in range(4):
                project(2, 4, 2, XH, XL, m["x_lo"] if j == 0 else None)
            m["x_lo"].next(DC)
            mlp()
            total(7)

        @block.scalar
        def _(act):
            b = Book(sems)
            m = b.m

            def upper(upto):
                while b.ahead < min(upto, NU):
                    u, s, i = b.ahead, b.ahead % NSLOT, b.du * b.state.i if b.du else 0
                    act.wait_ge(raw_in[s], 16 * (u // NSLOT + 1) + (16 * (b.du // NSLOT) * b.state.i if b.du else 0))
                    if u >= NSLOT:
                        act.wait_ge(sems["used"], u - NSLOT + 1 + i)
                    nc.scalar.activation(WH[:, s, :], raw[:, s, :], ACT.Copy).then_inc(*m["whi"].tick())
                    b.ahead += 1

            def landed(nu, nt, j):
                return (sems["used"], units(b, b.u, nu)) if j == nt - 1 else m["tile_done"].upto(j + 1)

            def close(nu, nt):
                b.u += nu
                b.t += nt
                m["tile_done"].n += nt - 1
                m["tile_free"].n += nt

            def square(c, src, n):
                if c == 0:
                    if m["norm_sum"].n:
                        act.wait_ge(*m["norm_sum"].upto())
                    nc.scalar.activation(acc[:, :], src, ACT.Square).then_inc(*m["sq_done"].tick())
                else:
                    if m["acc_add"].n >= 2:
                        act.wait_ge(*m["acc_add"].upto(-1))
                    nc.scalar.activation(sq[:, m["acc_add"].n % 2, :], src, ACT.Square).then_inc(*m["sq_done"].tick())
                    m["acc_add"].next()

            def root(out, n):
                act.wait_ge(*m["norm_sum"].next())
                nc.scalar.activation(out, ps[:, 7, :], ACT.Sqrt, bias=small[:, 0:1], scale=1.0 / n)\
                  .then_inc(*m["norm_std"].tick())

            def split_h(gain, src_sem=None):
                for c in range(DC):
                    if src_sem is not None:
                        act.wait_ge(*src_sem.next())
                    if c == 0 and b.u:
                        act.wait_ge(sems["used"], b.u)
                    nc.scalar.activation(XH[:, c, :], h[:, c, :], ACT.Copy, scale=col(gain, c)).then_inc(*m["x_hi"].tick())
                    square(c, h[:, c, :], DC)

            act.dma_start(vec[:, :], io["vecs"]).then_inc(sems["vec_in"], 16)
            act.dma_start(qt[64:128, 1, :].bitcast(mybir.dt.int32), io["positions"].to_broadcast([64, S]))\
               .then_inc(sems["rope_in"], 16)
            act.dma_start(mask1, io["mask"]).then_inc(sems["mask_in"], 16)
            act.dma_start(ident[:, :], io["ident"]).then_inc(sems["ident_in"], 16)
            upper(NSLOT)
            act.wait_ge(sems["x_in"], 16)
            act.wait_ge(sems["vec_in"], 16)
            split_h("g_mix_pre")
            root(rstd[:, :], D)

            act.wait_ge(*m["ang_r2"].next())
            nc.scalar.activation(rope[64:128, :], gt[64:128, 1, :], ACT.Sin).then_inc(*m["rope_sin"].tick())

            def gates():
                for j in range(2):
                    act.wait_ge(*m["tile_free"].upto(j + 1))
                    nc.scalar.activation(gt[:, j, :], gt[:, j, :], ACT.Sigmoid).then_inc(*m["gt_sig"].tick())
                close(2, 2)

            upper(b.u + 4)
            close(2, 2)
            upper(b.u + 4)
            gates()
            upper(b.u + 4)
            for j in range(2):
                act.wait_ge(*m["tile_free"].upto(j + 1))
                square(j, qkv[:, j, :], 3)
            close(2, 2)
            upper(b.u + 4)
            act.wait_ge(*m["tile_free"].upto(1))
            square(2, qkv[:, 2, :], 3)
            close(2, 2)
            upper(b.u + 4)
            close(2, 2)
            root(V1[:, 0, :], QR)
            upper(b.u + 4)
            for j in range(2):
                act.wait_ge(*m["tile_free"].upto(j + 1))
                square(j, qkv[:, 3 + j, :], 2)
            close(2, 2)
            for c in range(3):
                act.wait_ge(*m["qkv_g"].next())
                nc.scalar.activation(HH[:, c, :], qkv[:, c, :], ACT.Copy).then_inc(*m["qkv_hi"].tick())
            upper(b.u + 4)
            gates()
            root(V1[:, 1, :], KVR)
            for c in range(3, 5):
                act.wait_ge(*m["qkv_g"].next())
                nc.scalar.activation(HH[:, c, :], qkv[:, c, :], ACT.Copy).then_inc(*m["qkv_hi"].tick())
            act.wait_ge(*m["kr_rope"].next())
            for hd in range(1, H1):
                nc.scalar.activation(khat[64:96, hd, :], khat[64:96, 0, :], ACT.Copy).then_inc(*m["kr_copy"].tick())

            for j in range(4):
                upper(b.u + 3)
                for t in range(2):
                    hd = 2 * j + t
                    act.wait_ge(*landed(1, 2, t))
                    if hd >= 2:
                        act.wait_ge(*m["q_lo"].upto(hd - 1))
                    nc.scalar.activation(qt[0:64, hd % 2, :], ps[0:64, (b.t + t) % 4, :], ACT.Copy)\
                      .then_inc(*m["qt_nope"].tick())
                    act.wait_ge(*m["qt_rope"].next())
                    nc.scalar.activation(XH[0:96, hd, :], qt[0:96, hd % 2, :], ACT.Copy).then_inc(*m["q_hi"].tick())
                close(1, 2)
            m["q_lo"].next(H1)
            upper(b.u + 4)
            for t in range(4):
                act.wait_ge(*landed(1, 4, t))
                nc.scalar.activation(khat[0:64, 2 * t, :], ps[0:64, (b.t + t) % 4, :], ACT.Copy).then_inc(*m["k_half"].tick())
            close(1, 4)
            close(1, 4)
            upper(b.u + 4)
            act.wait_ge(sems["used"], b.u)
            act.wait_ge(*m["kr_copy"].upto())
            for hd in range(H1):
                act.wait_ge(*m["tile_free"].upto(-8 + hd // 2 + 1))
                nc.scalar.activation(HH[0:96, hd, :], khat[0:96, hd, :], ACT.Copy).then_inc(*m["k_hi"].tick())

            def exponentials(n, job, scale):
                act.wait_ge(*m["neg_max"].next())
                for qs in range(TT):
                    a = job.p(n)[:, POFF[qs]:POFF[qs] + P * (qs + 1)]
                    k = 8 * (n % 2) + qs
                    nc.scalar.activation(a, a, ACT.Exp, bias=small[:, NMX + k:NMX + k + 1], scale=scale,
                                         accum_out=small[:, SUM + k:SUM + k + 1]).then_inc(*m["p_exp"].tick())

            def copy_transposed(n, job):
                for g, (at, w) in enumerate(((0, 512), (512, 512), (1024, 256))):
                    act.wait_ge(*m["t_done"].next())
                    if g == 0 and n >= 2:
                        act.wait_ge(*m["o_done"].upto(n - 1))
                    nc.scalar.activation(job.pt(n)[:, at:at + w], ps[:, TBANK[g], 0:w], ACT.Copy)\
                      .then_inc(*m["pt_act"].tick())

            def head_pair_out(pair, out):
                act.wait_ge(*m["o_done"].upto(2 * pair + 2))
                nc.scalar.activation(out, ps[:, 6, :], ACT.Copy).then_inc(*m["o_out"].tick())

            act.wait_ge(*m["k_lo"].next(H1))
            for n in range(H1 + 2):
                if n >= 5 and n % 2:
                    head_pair_out((n - 5) // 2, O1[:, (n - 5) // 2, :])
                if n >= 2:
                    copy_transposed(n - 2, JOBS1[n - 2])
                if n < H1:
                    exponentials(n, JOBS1[n], SC1)
            head_pair_out(3, O1[:, 3, :])
            m["o_done"].next(H1)

            act.dma_start(xp, io["pT"].rearrange("(c p) n -> p c n", p=P)).then_inc(sems["p_in"], 16)
            act.wait_ge(*m["s_done"].next(3 * H1))
            for c in range(4):
                act.wait_ge(*m["o_out"].upto(c - 3))
                nc.scalar.activation(XH[:, c, :], O1[:, c, :], ACT.Copy).then_inc(*m["x_hi"].tick())
            m["conv_xc"].next(4)
            m["acc_add"].next(3)
            m["norm_sum"].next()
            for c in range(4):
                act.wait_ge(*m["conv_xc"].upto(c - 3))
                square(c, cacc[:, c, :], CC)
            root(rstd[:, :], CC)
            for c in range(4):
                act.wait_ge(*m["conv_xn"].next())
                nc.scalar.activation(cacc[:, c, :], cacc[:, c, :], ACT.Silu, bias=col("conv_ln_b", c),
                                     scale=col("conv_ln_g", c)).then_inc(*m["conv_act"].tick())
            for c in range(4):
                act.wait_ge(*m["conv_act"].upto(c - 3))
                nc.scalar.activation(XH[:, 4 + c, :], cacc[:, c, :], ACT.Copy).then_inc(*m["x_hi"].tick())
            for j in range(4):
                upper(b.u + 4)
                for t in range(2):
                    act.wait_ge(*m["tile_free"].upto(t + 1))
                    square(2 * j + t, Y[:, 2 * j + t, :], D)
                close(2, 2)
            root(rstd[:, :], D)

            act.wait_ge(sems["p_in"], 16)
            for c in range(2):
                nc.scalar.activation(HH[:, c, :], xp[:, c, :], ACT.Copy).then_inc(*m["hid_hi"].tick())
            for j in range(2):
                upper(b.u + 3)
                for t in range(4):
                    act.wait_ge(*m["tile_free"].upto(t + 1))
                    square(4 * j + t, ple[:, 4 * j + t, :], D)
                close(1, 4)
            root(up[:, 0, :], D)
            split_h("g_ffn_pre", m["h_upd"])
            root(rstd[:, :], D)

            def ffn_up(pairs, par):
                for pr in range(pairs):
                    upper(b.u + 4)
                    for j in range(2):
                        act.wait_ge(*m["ffn_g"].next())
                        nc.scalar.activation(gc_[:, j, :], gc_[:, j, :], ACT.Gelu_apprx_tanh).then_inc(*m["ffn_gelu"].tick())
                    close(2, 2)
                    upper(b.u + 4)
                    for j in range(2):
                        act.wait_ge(*m["hid_s"].next())
                        nc.scalar.activation(HH[:, 4 * par + 2 * pr + j, :], ftmp[:, j, :], ACT.Copy)\
                          .then_inc(*m["hid_hi"].tick())
                    close(2, 2)

            def down_rest(n, nt):
                for _ in range(n):
                    upper(b.u + 3)
                    close(1, nt)

            ffn_up(2, 0)
            upper(b.u + 3)
            lead = b.ahead - b.u
            with b.turns(act, 2, 24, dict(whi=24, tile_done=16, tile_free=32, ffn_g=8, ffn_gelu=8, hid_s=8, hid_hi=8)):
                for par in range(2):
                    ffn_up(2, 1 - par)
                    down_rest(4, 2)
                upper(b.u + lead)
            ffn_up(1, 1)
            down_rest(4, 2)
            for j in range(2):
                upper(b.u + 3)
                for t in range(4):
                    act.wait_ge(*m["tile_free"].upto(t + 1))
                    square(4 * j + t, Y[:, 4 * j + t, :], D)
                close(1, 4)
            root(rstd[:, :], D)

            for c in range(DC):
                act.wait_ge(*m["h_upd"].next())
                nc.scalar.activation(XH[:, c, :], h[:, c, :], ACT.Copy).then_inc(*m["x_hi"].tick())

            def split_chunk(gain, c):
                if gain is not None:
                    nc.scalar.activation(HH[:, c, :], h[:, c, :], ACT.Copy, scale=col(gain, c)).then_inc(*m["x_hi"].tick())
                square(c, h[:, c, :], DC)

            for j in range(5):
                if j < 4:
                    upper(b.u + 4)
                    for t in range(2):
                        act.wait_ge(*landed(2, 2, t))
                        nc.scalar.activation(ps[:, (b.t + t) % 4, :], ps[:, (b.t + t) % 4, :], ACT.Sigmoid)\
                          .then_inc(*m["ple_s"].tick())
                    close(2, 2)
                if j >= 1:
                    for t in range(2):
                        act.wait_ge(*m["h_upd"].next())
                        split_chunk("norm_mix_0", 2 * j - 2 + t)
            root(rstd[:, :], D)
            act.dma_start(ohs[0:33, :], io["onehots"]).then_inc(sems["onehot_in"], 16)
            act.dma_start(relb[0:33, :], io["relb"]).then_inc(sems["relb_in"], 16)
            act.dma_start(w2s, io["w2"]).then_inc(sems["w2_in"], 16)

            for j in range(4):
                upper(b.u + 4)
                close(2, 2)
                upper(b.u + 4)
                close(2, 2)
                upper(b.u + 4)
                for t in range(2):
                    act.wait_ge(*m["y_ok"].next())
                    nc.scalar.activation(XH[:, 2 * j + t, :], ay[:, t, :], ACT.Copy).then_inc(*m["x_hi"].tick())
                close(2, 2)
                if j == 1:
                    act.wait_ge(*m["tab_out"].next(2))
                    act.dma_start(io["tab"], tabs[0:H2, :].unsqueeze(1).to_broadcast([H2, P, 640]))\
                       .then_inc(sems["tab_st"], 16)

            def residual(n, nu, nt, gain):
                for j in range(n):
                    upper(b.u + (4 if nu == 2 else 3))
                    for t in range(nt):
                        act.wait_ge(*m["tile_free"].upto(t + 1))
                        split_chunk(gain, nt * j + t)
                    close(nu, nt)

            residual(4, 2, 2, "norm_mlp_0")

            def mlp(gain):
                root(rstd[:, :], D)

                def up_(par):
                    for pr in range(2):
                        upper(b.u + 4)
                        for t in range(2):
                            act.wait_ge(*m["tile_free"].upto(t + 1))
                            nc.scalar.activation(XH[:, 4 * par + 2 * pr + t, :], rt[:, 2 * pr + t, :], ACT.Square)\
                              .then_inc(*m["hid_hi"].tick())
                        close(2, 2)

                up_(0)
                upper(b.u + 3)
                lead = b.ahead - b.u
                with b.turns(act, 3, 16, dict(whi=16, tile_done=12, tile_free=24, hid_hi=8)):
                    for par in range(2):
                        up_(1 - par)
                        down_rest(4, 2)
                    upper(b.u + lead)
                up_(1)
                down_rest(4, 2)
                residual(4, 1, 2, gain)

            mlp("kv_norm")

            root(rstd[:, :], D)
            upper(b.u + 4)
            close(2, 2)
            upper(b.u + 4)
            close(2, 2)
            for i in range(2):
                act.wait_ge(*m["kr_pad"].next(10))
                nc.scalar.activation(FH[i], KR[i], ACT.Copy).then_inc(*m["kr_hi"].tick())
            for _ in range(2):
                upper(b.u + 4)
                close(2, 2)
                upper(b.u + 4)
                close(2, 4)
            act.wait_ge(sems["used"], b.u)
            for i in range(2):
                upper(b.u + 4)
                if i == 0:
                    for c in range(DC):
                        nc.scalar.activation(HH[:, c, :], h[:, c, :], ACT.Copy, scale=col("norm_mix_1", c))\
                          .then_inc(*m["x_hi"].tick())
                for t in range(2):
                    act.wait_ge(*m["tile_free"].upto(t + 1))
                    nc.scalar.activation(hid[:, 2 * i + t, :], pre[:, t, 0:P], ACT.Silu, bias=pre[:, t, P:P + 1])\
                      .then_inc(*m["silu_ok"].tick())
                close(4, 2)
            upper(b.u + 4)
            act.wait_ge(*m["cmp_done"].next())
            nc.scalar.activation(KCH[:, :], ps[:, 6, 0:P], ACT.Copy).then_inc(*m["kc_hi"].tick())
            for j in range(4):
                upper(b.u + 4)
                for t in range(2):
                    act.wait_ge(*m["tile_free"].upto(t + 1))
                    nc.scalar.activation(XH[:, 2 * j + t, :], qst[:, (2 * j + t) % 4, :], ACT.Copy).then_inc(*m["q_hi"].tick())
                close(2, 2)
            upper(b.u + 3)
            act.wait_ge(*m["tile_free"].upto(4))
            nc.scalar.activation(GT, GT, ACT.Sigmoid).then_inc(*m["gate_s"].tick())
            close(1, 4)
            m["tile_free"].n += 2 * TT
            b.t = 0
            act.wait_ge(*m["kv_ok"].next(16))
            for c in range(2 * GR):
                nc.scalar.activation(HH[:, c, :], K32[:, c, :], ACT.Copy).then_inc(*m["krep_hi"].tick())
            upper(b.u + 4)
            for t in range(TT):
                act.wait_ge(*m["c_sub"].next())
                nc.scalar.activation(L[:, t, :], L[:, t, :], ACT.Exp).then_inc(*m["c_exp"].tick())
            for t in range(TT):
                act.wait_ge(*m["c_tr"].next())
                nc.scalar.activation(PCT[:, :, t * P:(t + 1) * P],
                                     ps[:, 4 + t % 2, :].rearrange("p (i q) -> p i q", i=HG), ACT.Copy)\
                  .then_inc(*m["c_pt"].tick())
            act.wait_ge(*m["krep_lo"].next(2 * GR))

            def pair_out(pair):
                act.wait_ge(*m["o_done"].upto(4 * pair + 4))
                nc.scalar.activation(O2[:, pair, :], ps[:, 6, :], ACT.Copy).then_inc(*m["o_out"].tick())
                act.wait_ge(*m["o_out"].upto())
                nc.scalar.activation(XH[:, pair, :], O2[:, pair, :], ACT.Copy).then_inc(*m["x_hi"].tick())

            NJ = 2 * H2
            for n in range(NJ + 2):
                if n >= 7 and n % 4 == 3:
                    pair_out((n - 7) // 4)
                if n >= 2:
                    copy_transposed(n - 2, JOBS2[n - 2])
                if n < NJ:
                    exponentials(n, JOBS2[n], 1.0)
            pair_out(DC - 1)
            m["o_done"].next(NJ)
            residual(4, 2, 2, "norm_mlp_1")
            mlp(None)
            root(rstd[:, :], D)

        @block.vector
        def _(dve):
            b = Book(sems)
            m = b.m
            V = nc.vector

            def landed(nu, nt, j):
                return (sems["used"], units(b, b.u, nu)) if j == nt - 1 else m["tile_done"].upto(j + 1)

            def bank(j, n=S):
                return ps[:, (b.t + j) % 4, 0:n]

            def close(nu, nt):
                b.u += nu
                b.t += nt
                m["tile_done"].n += nt - 1

            def add_square(c):
                m["sq_done"].next()
                if c:
                    dve.wait_ge(*m["sq_done"].upto())
                    if c > 1:
                        dve.wait_ge(*m["acc_add"].upto())
                    V.tensor_tensor(acc[:, :], acc[:, :], sq[:, m["acc_add"].n % 2, :], ADD).then_inc(*m["acc_add"].tick())

            def invert(x):
                m["norm_sum"].next()
                dve.wait_ge(*m["norm_std"].next())
                V.reciprocal(x, x).then_inc(*m["norm_inv"].tick())

            def lower_h(gain, c):
                dve.wait_ge(*m["x_hi"].next())
                V.scalar_tensor_tensor(XL[:, c, :], h[:, c, :], col(gain, c), XH[:, c, :].bitcast(f32), MUL, SUB)\
                 .then_inc(*m["x_lo"].tick())

            def lower(out, src, up_, hi, lo):
                dve.wait_ge(*hi.next())
                V.tensor_tensor(out, src, up_.bitcast(f32), SUB).then_inc(*lo.tick())

            V.memset(small[:, :], EPS).then_inc(*m["taps"].tick())
            dve.wait_ge(sems["vec_in"], 16)
            dve.wait_ge(sems["rope_in"], 16)
            lanes = slice(64, 128)
            ang, red, whole = gt[lanes, 0, :], gt[lanes, 1, :], qt[lanes, 0, :]
            V.tensor_copy(ang, qt[lanes, 1, :].bitcast(mybir.dt.int32)).then_inc(*m["ang"].tick())
            dve.wait_ge(*m["ang"].upto())
            V.tensor_scalar(ang, ang, vec[lanes, VO["freq"]:VO["freq"] + 1], None, MUL).then_inc(*m["ang"].tick())
            dve.wait_ge(*m["ang"].upto())
            V.tensor_scalar(red, ang, 1 / (2 * math.pi), vec[lanes, VO["cosine"]:VO["cosine"] + 1], MUL, ADD)\
             .then_inc(*m["ang"].tick())
            dve.wait_ge(*m["ang"].upto())
            V.tensor_copy(whole.bitcast(mybir.dt.int32), red).then_inc(*m["ang"].tick())
            dve.wait_ge(*m["ang"].upto())
            V.tensor_copy(whole, whole.bitcast(mybir.dt.int32)).then_inc(*m["ang"].tick())
            for n, part in enumerate(TURN):
                dve.wait_ge(*m["ang"].upto())
                V.scalar_tensor_tensor(red, whole, -part, ang if n == 0 else red, MUL, ADD).then_inc(*m["ang"].tick())
            dve.wait_ge(*m["ang"].upto())
            V.tensor_scalar(red, red, vec[lanes, VO["quarter"]:VO["quarter"] + 1], None, ADD).then_inc(*m["ang"].tick())
            dve.wait_ge(*m["ang"].upto())
            V.tensor_scalar(red, red, 3.1415925, -3.1415925, ALU.min, MAX).then_inc(*m["ang_r2"].tick())

            for c in range(DC):
                lower_h("g_mix_pre", c)
                add_square(c)
            dve.wait_ge(*m["rope_sin"].next())
            V.tensor_scalar(rope[lanes, :], rope[lanes, :], vec[lanes, VO["sign"]:VO["sign"] + 1], None, MUL)\
             .then_inc(*m["ang"].tick())
            invert(rstd[:, :])

            def taps():
                for first in (0, 2):
                    for k in range(CW):
                        for c in (first, first + 1):
                            yield k, c

            steps = taps()
            base = m["taps"].n

            def convolve(n):
                for _ in range(n):
                    k, c = next(steps, (None, None))
                    if k is None:
                        return
                    if k:
                        dve.wait_ge(*m["taps"].upto(-1))
                    w = vec[:, VO["conv_w"] + 4 * k + c:VO["conv_w"] + 4 * k + c + 1]
                    if k == 0:
                        V.tensor_scalar(cacc[:, c, :], cpad[:, c, 0:S], w, col("conv_b", c), MUL, ADD)\
                         .then_inc(*m["taps"].tick())
                    else:
                        V.scalar_tensor_tensor(cacc[:, c, :], cpad[:, c, k:k + S], w, cacc[:, c, :], MUL, ADD)\
                         .then_inc(*m["taps"].tick())

            def channels(c0):
                for j in range(2):
                    dve.wait_ge(*landed(2, 2, j))
                    V.tensor_tensor(cpad[:, c0 + j, CW - 1:PADW], bank(j), rstd[:, :], MUL).then_inc(*m["tile_free"].tick())
                close(2, 2)

            def gates(c0):
                for j in range(2):
                    dve.wait_ge(*landed(2, 2, j))
                    V.tensor_tensor(gt[:, j, :], bank(j), rstd[:, :], MUL).then_inc(*m["tile_free"].tick())
                close(2, 2)
                for j in range(2):
                    dve.wait_ge(*m["gt_sig"].next())
                    V.tensor_tensor(cpad[:, c0 + j, CW - 1:PADW], cpad[:, c0 + j, CW - 1:PADW], gt[:, j, :], MUL)\
                     .then_inc(*m["c_ok"].tick())
                dve.wait_ge(*m["c_ok"].upto())

            def low_rank(c, j):
                dve.wait_ge(*landed(2, 2, j))
                V.tensor_tensor(qkv[:, c, :], bank(j), rstd[:, :], MUL).then_inc(*m["tile_free"].tick())

            def normalised(c, gain, k, root_):
                V.scalar_tensor_tensor(qkv[:, c, :], qkv[:, c, :], col(gain, k), root_, MUL, MUL).then_inc(*m["qkv_g"].tick())

            dve.wait_ge(*m["norm_inv"].upto())
            dve.wait_ge(sems["const_ok"], 2)
            channels(0)
            gates(0)
            for j in range(2):
                low_rank(j, j)
                add_square(j)
            close(2, 2)
            convolve(4)
            low_rank(2, 0)
            add_square(2)
            dve.wait_ge(*landed(2, 2, 1))
            V.tensor_tensor(qt[lanes, 1, :], ps[lanes, (b.t + 1) % 4, :], rstd[lanes, :], MUL).then_inc(*m["tile_free"].tick())
            dve.wait_ge(*m["tile_free"].upto())
            dve.wait_ge(*m["ang"].upto())
            V.tensor_tensor(qt[64:96, 0, :], qt[96:128, 1, :], rope[96:128, :], MUL).then_inc(*m["kr_part"].tick())
            V.tensor_tensor(khat[64:96, 0, :], qt[64:96, 1, :], rope[64:96, :], MUL).then_inc(*m["kr_part"].tick())
            dve.wait_ge(*m["kr_part"].upto())
            V.tensor_tensor(khat[64:96, 0, :], khat[64:96, 0, :], qt[64:96, 0, :], ADD).then_inc(*m["kr_rope"].tick())
            close(2, 2)
            convolve(10)
            channels(2)
            convolve(4)
            invert(V1[:, 0, :])
            dve.wait_ge(*m["norm_inv"].upto())
            for c in range(3):
                normalised(c, "g_q_a", c, V1[:, 0, :])
            for j in range(2):
                low_rank(3 + j, j)
                add_square(j)
            close(2, 2)
            for c in range(3):
                lower(HL[:, c, :], qkv[:, c, :], HH[:, c, :], m["qkv_hi"], m["qkv_lo"])
            convolve(6)
            gates(2)
            invert(V1[:, 1, :])
            dve.wait_ge(*m["norm_inv"].upto())
            for c in range(3, 5):
                normalised(c, "g_kv_a", c - 3, V1[:, 1, :])
            for c in range(3, 5):
                lower(HL[:, c, :], qkv[:, c, :], HH[:, c, :], m["qkv_hi"], m["qkv_lo"])

            def query_low(hd):
                lower(XL[0:96, hd, :], qt[0:96, hd % 2, :], XH[0:96, hd, :], m["q_hi"], m["q_lo"])

            for j in range(4):
                for t in range(2):
                    hd = 2 * j + t
                    dve.wait_ge(*landed(1, 2, t))
                    bk = ps[:, (b.t + t) % 4, :]
                    if hd >= 2:
                        dve.wait_ge(*m["q_lo"].upto())
                    V.tensor_tensor(qt[64:96, hd % 2, :], bk[96:128], rope[96:128, :], MUL).then_inc(*m["qt_r"].tick())
                    dve.wait_ge(*m["qt_nope"].next())
                    V.tensor_tensor(gt[64:96, hd % 2, :], bk[64:96], rope[64:96, :], MUL).then_inc(*m["tile_free"].tick())
                    dve.wait_ge(*m["qt_r"].upto())
                    dve.wait_ge(*m["tile_free"].upto())
                    V.tensor_tensor(qt[64:96, hd % 2, :], qt[64:96, hd % 2, :], gt[64:96, hd % 2, :], ADD)\
                     .then_inc(*m["qt_rope"].tick())
                    convolve(1)
                    if hd:
                        query_low(hd - 1)
                close(1, 2)
            query_low(H1 - 1)
            for t in range(4):
                dve.wait_ge(*landed(1, 4, t))
                dve.wait_ge(*m["k_half"].next())
                V.tensor_copy(khat[0:64, 2 * t + 1, :], ps[64:128, (b.t + t) % 4, :]).then_inc(*m["tile_free"].tick())
            close(1, 4)
            for t in range(4):
                dve.wait_ge(*landed(1, 4, t))
                V.tensor_copy(V1[:, t, :], bank(t)).then_inc(*m["tile_free"].tick())
            close(1, 4)
            for hd in range(H1):
                lower(HL[0:96, hd, :], khat[0:96, hd, :], HH[0:96, hd, :], m["k_hi"], m["k_lo"])

            def logits(n, job):
                if n >= 3:
                    dve.wait_ge(*m["t_done"].upto(3 * (n - 2)))
                for qs, bk, at in SCORES:
                    w = P * (qs + 1)
                    k = 8 * (n % 2) + qs
                    dve.wait_ge(*(m["s_done"].upto() if qs == 1 else m["s_done"].next()))
                    V.tensor_tensor_reduce(out=job.p(n)[:, POFF[qs]:POFF[qs] + w],
                                           in0=ps[:, (3 * n + bk) % 4, at:at + w], in1=job.bias[:, S - w:S], scale=1.0,
                                           scalar=-3.0e38, op0=ADD, op1=MAX,
                                           accum_out=small[:, MXC + k:MXC + k + 1]).then_inc(*m["l_done"].tick())
                k = 8 * (n % 2)
                dve.wait_ge(*m["l_done"].upto())
                V.tensor_scalar(small[:, NMX + k:NMX + k + 4], small[:, MXC + k:MXC + k + 4], -job.scale, None, MUL)\
                 .then_inc(*m["neg_max"].tick())

            def normalise(n, job):
                k = 8 * (n % 2)
                m["p_exp"].next(4)
                dve.wait_ge(*m["p_exp"].upto())
                V.reciprocal(small[:, INV + k:INV + k + 4], small[:, SUM + k:SUM + k + 4]).then_inc(*m["p_inv"].tick())
                if job.gate is not None:
                    dve.wait_ge(*m["p_inv"].upto())
                    V.tensor_tensor(small[:, INV + k:INV + k + 4], small[:, INV + k:INV + k + 4], job.gate, MUL)\
                     .then_inc(*m["p_inv"].tick())
                dve.wait_ge(*m["p_inv"].upto())
                for qs in range(TT):
                    a = job.p(n)[:, POFF[qs]:POFF[qs] + P * (qs + 1)]
                    V.tensor_scalar(a, a, small[:, INV + k + qs:INV + k + qs + 1], None, MUL).then_inc(*m["p_norm"].tick())

            dve.wait_ge(sems["mask_in"], 16)
            for n in range(H1 + 1):
                if n < H1:
                    logits(n, JOBS1[n])
                if n >= 1:
                    normalise(n - 1, JOBS1[n - 1])
                convolve(9)
            convolve(4 * CW)
            m["t_done"].next(3 * H1)

            for c in range(4):
                m["o_out"].next()
                lower(XL[:, c, :], O1[:, c, :], XH[:, c, :], m["x_hi"], m["x_lo"])
            dve.wait_ge(*m["taps"].upto())
            dve.wait_ge(*m["norm_sum"].upto())
            for c in range(1, 4):
                V.tensor_tensor(acc[:, :], cacc[:, 0, :] if c == 1 else acc[:, :], cacc[:, c, :], ADD)\
                 .then_inc(*m["acc_add"].tick())
                dve.wait_ge(*m["acc_add"].upto())
            dve.wait_ge(*m["norm_sum"].next())
            for c in range(4):
                V.scalar_tensor_tensor(cacc[:, c, :], ps[:, 7, :], -1.0 / CC, cacc[:, c, :], MUL, ADD)\
                 .then_inc(*m["conv_xc"].tick())
            for c in range(4):
                add_square(c)
            invert(rstd[:, :])
            dve.wait_ge(*m["norm_inv"].upto())
            for c in range(4):
                V.tensor_tensor(cacc[:, c, :], cacc[:, c, :], rstd[:, :], MUL).then_inc(*m["conv_xn"].tick())
            for c in range(4):
                lower(XL[:, 4 + c, :], cacc[:, c, :], XH[:, 4 + c, :], m["x_hi"], m["x_lo"])
            for j in range(4):
                for t in range(2):
                    dve.wait_ge(*landed(2, 2, t))
                    V.tensor_copy(Y[:, 2 * j + t, :], bank(t)).then_inc(*m["tile_free"].tick())
                    if t or j:
                        add_square(2 * j + t - 1)
                close(2, 2)
            add_square(DC - 1)

            def add_normalised(gain, c, src):
                V.scalar_tensor_tensor(src[:, c, :], src[:, c, :], col(gain, c), rstd[:, :], MUL, MUL).then_inc(*m["y_tmp"].tick())
                dve.wait_ge(*m["y_tmp"].upto())
                V.tensor_tensor(h[:, c, :], h[:, c, :], src[:, c, :], ADD).then_inc(*m["h_upd"].tick())

            dve.wait_ge(sems["p_in"], 16)
            for c in range(2):
                lower(HL[:, c, :], xp[:, c, :], HH[:, c, :], m["hid_hi"], m["hid_lo"])
            for j in range(2):
                for t in range(4):
                    dve.wait_ge(*landed(1, 4, t))
                    V.tensor_copy(ple[:, 4 * j + t, :], bank(t)).then_inc(*m["tile_free"].tick())
                    if t or j:
                        add_square(4 * j + t - 1)
                close(1, 4)
            add_square(DC - 1)
            invert(rstd[:, :])
            dve.wait_ge(*m["norm_inv"].upto())
            for c in range(DC):
                add_normalised("g_mix_post", c, Y)
                lower_h("g_ffn_pre", c)
                add_square(c)
            invert(up[:, 0, :])
            dve.wait_ge(*m["norm_inv"].upto())
            for c in range(DC):
                V.scalar_tensor_tensor(ple[:, c, :], ple[:, c, :], col("g_ple", c), up[:, 0, :], MUL, MUL)\
                 .then_inc(*m["e_g"].tick())
            for c in range(DC):
                V.memset(Y[:, c, :], 0.0).then_inc(*m["y_out"].tick())
            V.memset(gpad[:, :, 0:2], 0.0).then_inc(*m["y_out"].tick())
            invert(rstd[:, :])
            dve.wait_ge(*m["norm_inv"].upto())
            dve.wait_ge(*m["y_out"].upto())

            def dw(k, f):
                o = VO["ffn_dw_b"] if k == 3 else VO["ffn_dw_w"] + k * FC
                return vec[:, bass.ds(o + f, 1)] if not isinstance(f, int) else vec[:, o + f:o + f + 1]

            def ffn_up(f0, pairs, par):
                for pr in range(pairs):
                    f = [f0 + 2 * pr + j for j in range(2)]
                    for j in range(2):
                        dve.wait_ge(*landed(2, 2, j))
                        V.tensor_tensor(gpad[:, j, 2:S + 2], bank(j), rstd[:, :], MUL).then_inc(*m["tile_free"].tick())
                    close(2, 2)
                    dve.wait_ge(*m["tile_free"].upto())
                    for j in range(2):
                        V.tensor_scalar(gc_[:, j, :], gpad[:, j, 2:S + 2], dw(2, f[j]), dw(3, f[j]), MUL, ADD)\
                         .then_inc(*m["ffn_t"].tick())
                    for j in range(2):
                        dve.wait_ge(*m["ffn_t"].upto(j - 1))
                        V.scalar_tensor_tensor(gc_[:, j, :], gpad[:, j, 1:S + 1], dw(1, f[j]), gc_[:, j, :], MUL, ADD)\
                         .then_inc(*m["ffn_u"].tick())
                    for j in range(2):
                        dve.wait_ge(*m["ffn_u"].upto(j - 1))
                        V.scalar_tensor_tensor(gc_[:, j, :], gpad[:, j, 0:S], dw(0, f[j]), gc_[:, j, :], MUL, ADD)\
                         .then_inc(*m["ffn_g"].tick())
                    for j in range(2):
                        dve.wait_ge(*landed(2, 2, j))
                        V.tensor_tensor(up[:, j, :], bank(j), rstd[:, :], MUL).then_inc(*m["tile_free"].tick())
                    close(2, 2)
                    dve.wait_ge(*m["tile_free"].upto())
                    for j in range(2):
                        dve.wait_ge(*m["ffn_gelu"].next())
                        V.tensor_tensor(ftmp[:, j, :], gc_[:, j, :], up[:, j, :], MUL).then_inc(*m["hid_s"].tick())
                    for j in range(2):
                        s = 4 * par + 2 * pr + j
                        lower(HL[:, s, :], ftmp[:, j, :], HH[:, s, :], m["hid_hi"], m["hid_lo"])

            def add_downs(n, nt, squares=False):
                for j in range(n):
                    for t in range(nt):
                        dve.wait_ge(*landed(1, nt, t))
                        dve.wait_ge(*m["tile_free"].upto())
                        V.tensor_tensor(Y[:, nt * j + t, :], Y[:, nt * j + t, :], bank(t), ADD).then_inc(*m["tile_free"].tick())
                        if squares and (t or j):
                            add_square(nt * j + t - 1)
                    close(1, nt)
                if squares:
                    add_square(DC - 1)

            ffn_up(0, 2, 0)
            with b.turns(dve, 2, 24, dict(tile_done=16, tile_free=32, ffn_t=8, ffn_u=8, ffn_g=8, ffn_gelu=8, hid_s=8,
                                          hid_hi=8, hid_lo=8)) as i:
                for par in range(2):
                    ffn_up(8 * i + 4 + 4 * par, 2, 1 - par)
                    add_downs(4, 2)
            ffn_up(20, 1, 1)
            add_downs(4, 2)
            add_downs(2, 4, True)
            invert(rstd[:, :])
            dve.wait_ge(*m["norm_inv"].upto())
            for c in range(DC):
                add_normalised("g_ffn_post", c, Y)
                dve.wait_ge(*m["x_hi"].next())
                V.tensor_tensor(XL[:, c, :], h[:, c, :], XH[:, c, :].bitcast(f32), SUB).then_inc(*m["x_lo"].tick())

            def lower_chunk(gain, c):
                if gain is not None:
                    dve.wait_ge(*m["x_hi"].next())
                    V.scalar_tensor_tensor(HL[:, c, :], h[:, c, :], col(gain, c), HH[:, c, :].bitcast(f32), MUL, SUB)\
                     .then_inc(*m["x_lo"].tick())
                add_square(c)

            for j in range(5):
                if j < 4:
                    for t in range(2):
                        c = 2 * j + t
                        dve.wait_ge(*m["ple_s"].next())
                        V.tensor_tensor(ptmp[:, t, :], bank(t), ple[:, c, :], MUL).then_inc(*m["tile_free"].tick())
                        dve.wait_ge(*m["tile_free"].upto())
                        V.tensor_tensor(h[:, c, :], h[:, c, :], ptmp[:, t, :], ADD).then_inc(*m["h_upd"].tick())
                    close(2, 2)
                    dve.wait_ge(*m["h_upd"].upto())
                if j >= 1:
                    for t in range(2):
                        lower_chunk("norm_mix_0", 2 * j - 2 + t)
            V.memset(apad[:, :, 0:2], 0.0).then_inc(*m["v_ok"].tick())
            invert(rstd[:, :])
            dve.wait_ge(*m["norm_inv"].upto())
            V.tensor_tensor(rr, rstd[:, :], rstd[:, :], MUL).then_inc(*m["r_ok"].tick())
            dve.wait_ge(*m["r_ok"].upto())

            def copy_tables():
                for k, w in ((0, 512), (1, 128)):
                    dve.wait_ge(*m["tab_done"].next())
                    V.tensor_copy(tabs[0:H2, 512 * k:512 * k + w], ps[0:H2, 4 + k, 0:w]).then_inc(*m["tab_out"].tick())
                for t in range(TT):
                    dve.wait_ge(*m["tab_done"].next())
                    V.tensor_copy(bcs[:, t, :], ps[:, 4 + t % 2, :]).then_inc(*m["tab_out"].tick())

            for j in range(4):
                for t in range(2):
                    dve.wait_ge(*landed(2, 2, t))
                    V.tensor_tensor(acs[:, t, :], bank(t), rr, MUL).then_inc(*m["tile_free"].tick())
                close(2, 2)
                dve.wait_ge(*m["tile_free"].upto())
                if j:
                    dve.wait_ge(*m["cu_t"].upto())
                for t in range(2):
                    dve.wait_ge(*landed(2, 2, t))
                    V.tensor_tensor(apad[:, t, 2:S + 2], bank(t), acs[:, t, :], MUL).then_inc(*m["tile_free"].tick())
                close(2, 2)
                dve.wait_ge(*m["tile_free"].upto())
                dve.wait_ge(*m["v_ok"].upto())
                if j:
                    dve.wait_ge(*m["y_ok"].upto())
                for k in (2, 1, 0):
                    for t in range(2):
                        w = col("a_conv_w", k * DC + 2 * j + t)
                        if k == 2:
                            V.tensor_scalar(act_[:, t, :], apad[:, t, 2:S + 2], w, None, MUL).then_inc(*m["cu_t"].tick())
                        else:
                            dve.wait_ge(*m["cu_t"].upto(-1))
                            V.scalar_tensor_tensor(act_[:, t, :], apad[:, t, k:k + S], w, act_[:, t, :], MUL, ADD)\
                             .then_inc(*m["cu_t"].tick())
                dve.wait_ge(*m["cu_t"].upto())
                for t in range(2):
                    dve.wait_ge(*landed(2, 2, t))
                    V.tensor_tensor(abs_[:, t, :], bank(t), rstd[:, :], MUL).then_inc(*m["tile_free"].tick())
                close(2, 2)
                dve.wait_ge(*m["tile_free"].upto())
                if j:
                    dve.wait_ge(*m["x_lo"].upto())
                for t in range(2):
                    V.tensor_tensor(ay[:, t, :], act_[:, t, :], abs_[:, t, :], MUL).then_inc(*m["y_ok"].tick())
                for t in range(2):
                    lower(XL[:, 2 * j + t, :], ay[:, t, :], XH[:, 2 * j + t, :], m["x_hi"], m["x_lo"])
                if j == 1:
                    copy_tables()

            def residual(n, nu, nt, gain):
                for j in range(n):
                    for t in range(nt):
                        c = nt * j + t
                        dve.wait_ge(*landed(nu, nt, t))
                        V.tensor_tensor(h[:, c, :], h[:, c, :], bank(t), ADD).then_inc(*m["tile_free"].tick())
                        if c:
                            lower_chunk(gain, c - 1)
                    close(nu, nt)
                dve.wait_ge(*m["tile_free"].upto())
                lower_chunk(gain, nt * n - 1)

            residual(4, 2, 2, "norm_mlp_0")

            def mlp(gain):
                invert(rstd[:, :])
                dve.wait_ge(*m["norm_inv"].upto())
                dve.wait_ge(*m["x_lo"].upto())

                def up_(par):
                    for pr in range(2):
                        for t in range(2):
                            dve.wait_ge(*landed(2, 2, t))
                            V.scalar_tensor_tensor(rt[:, 2 * pr + t, :], bank(t), 0.0, rstd[:, :], MAX, MUL)\
                             .then_inc(*m["tile_free"].tick())
                        close(2, 2)
                        dve.wait_ge(*m["tile_free"].upto())
                        for t in range(2):
                            V.tensor_tensor(st_[:, 2 * pr + t, :], rt[:, 2 * pr + t, :], rt[:, 2 * pr + t, :], MUL)\
                             .then_inc(*m["hid_s"].tick())
                        dve.wait_ge(*m["hid_s"].upto())
                        for t in range(2):
                            c = 4 * par + 2 * pr + t
                            lower(XL[:, c, :], st_[:, 2 * pr + t, :], XH[:, c, :], m["hid_hi"], m["hid_lo"])

                def down_():
                    for j in range(4):
                        for t in range(2):
                            c = 2 * j + t
                            dve.wait_ge(*landed(1, 2, t))
                            V.tensor_tensor(h[:, c, :], h[:, c, :], bank(t), ADD).then_inc(*m["tile_free"].tick())
                        close(1, 2)
                    dve.wait_ge(*m["tile_free"].upto())
                    dve.wait_ge(*m["hid_lo"].upto())

                up_(0)
                dve.wait_ge(*m["hid_lo"].upto())
                with b.turns(dve, 3, 16, dict(tile_done=12, tile_free=24, hid_hi=8, hid_s=8, hid_lo=8)):
                    for par in range(2):
                        up_(1 - par)
                        down_()
                up_(1)
                down_()
                residual(4, 1, 2, gain)

            mlp("kv_norm")

            dve.wait_ge(sems["tab_st"], 16)
            for i in range(2):
                V.memset(KR[i], 0.0).then_inc(*m["kr_ok"].tick())
            invert(rstd[:, :])
            dve.wait_ge(*m["norm_inv"].upto())
            dve.wait_ge(*m["kr_ok"].upto())
            dve.wait_ge(*m["hid_lo"].upto())
            for i, name in enumerate(("pe_k", "pe_v")):
                for t in range(2):
                    dve.wait_ge(*landed(2, 2, t))
                    for gi in range(2):
                        rows = slice(64 * gi, 64 * gi + 64)
                        for odd in range(2):
                            V.tensor_tensor(KR[i][64 * odd:64 * odd + 64, 2 * t + gi, 0:256],
                                            ps[rows, (b.t + t) % 4, odd::2], rstd[rows, odd::2], MUL)\
                             .then_inc(*m["kr_pad"].tick())
                    dve.wait_ge(*m["kr_pad"].upto())
                    V.tensor_copy(KR[i][:, 4, 8 * t:8 * t + 8], vec[:, VO[name] + 8 * t:VO[name] + 8 * t + 8])\
                     .then_inc(*m["kr_pad"].tick())
                    V.tensor_copy(small[:, 1:2], small[:, 0:1]).then_inc(*m["tile_free"].tick())
                close(2, 2)
            dve.wait_ge(*m["kr_pad"].upto())
            dve.wait_ge(*m["col_done"].next())
            V.tensor_copy(small[:, 80:84], ps[:, 6, 0:S:P]).then_inc(*m["col_ok"].tick())
            dve.wait_ge(*m["col_ok"].upto())
            for i in range(2):
                dve.wait_ge(*m["kr_hi"].next())
                V.tensor_tensor(FL[i], KR[i], FH[i].bitcast(f32), SUB).then_inc(*m["kr_lo"].tick())
            for br in range(2):
                for t in range(2):
                    dve.wait_ge(*landed(2, 2, t))
                    for gi in range(2):
                        rows = slice(64 * gi, 64 * gi + 64)
                        for half in range(2):
                            V.tensor_tensor(K32[64 * half:64 * half + 64, br * 4 + 2 * t + gi, :],
                                            ps[rows, (b.t + t) % 4, :], rstd[rows, :], MUL).then_inc(*m["kv_ok"].tick())
                    dve.wait_ge(*m["kv_ok"].upto())
                    V.tensor_copy(small[:, 1:2], small[:, 0:1]).then_inc(*m["tile_free"].tick())
                close(2, 2)
                for t in range(TT):
                    dve.wait_ge(*landed(2, 4, t))
                    V.tensor_scalar(V2[:, t, br * 256:br * 256 + 256], bank(t, 256), small[:, 80 + t:81 + t], None, MUL)\
                     .then_inc(*m["tile_free"].tick())
                close(2, 4)
            for i in range(2):
                if i == 0:
                    for c in range(DC):
                        dve.wait_ge(*m["x_hi"].next())
                        V.scalar_tensor_tensor(HL[:, c, :], h[:, c, :], col("norm_mix_1", c), HH[:, c, :].bitcast(f32),
                                               MUL, SUB).then_inc(*m["x_lo"].tick())
                for t in range(2):
                    dve.wait_ge(*landed(4, 2, t))
                    if i:
                        dve.wait_ge(*m["silu_ok"].next())
                    V.tensor_copy(pre[:, t, :], bank(t, 160)).then_inc(*m["tile_free"].tick())
                close(4, 2)
            dve.wait_ge(*m["kc_hi"].next())
            V.tensor_tensor(KCL[:, :], ps[:, 6, 0:P], KCH[:, :].bitcast(f32), SUB).then_inc(*m["kc_lo"].tick())
            dve.wait_ge(*m["cmp_done"].next(2))
            V.tensor_copy(VC, ps[:, 5, 0:HD]).then_inc(*m["vc_ok"].tick())
            for j in range(4):
                for t in range(2):
                    c = 2 * j + t
                    dve.wait_ge(*landed(2, 2, t))
                    if c >= 4:
                        dve.wait_ge(*m["q_lo"].upto(-2))
                    V.scalar_tensor_tensor(qst[:, c % 4, :], bank(t), SC2, rstd[:, :], MUL, MUL).then_inc(*m["tile_free"].tick())
                dve.wait_ge(*m["tile_free"].upto())
                for t in range(2):
                    c = 2 * j + t
                    lower(XL[:, c, :], qst[:, c % 4, :], XH[:, c, :], m["q_hi"], m["q_lo"])
                close(2, 2)
            for t in range(TT):
                dve.wait_ge(*landed(1, 4, t))
                V.tensor_scalar(GT[:, t, :], bank(t, 48), small[:, 80 + t:81 + t], None, MUL).then_inc(*m["tile_free"].tick())
            close(1, 4)
            dve.wait_ge(*m["gate_s"].next())
            V.tensor_scalar(GT[:, 0, 0:48:3], GT[:, 0, 0:48:3], col("has_any"), None, MUL).then_inc(*m["gate_ok"].tick())
            dve.wait_ge(*m["tab_out"].upto())
            def parity(x, t, r):
                return x[:, t, :].rearrange("p (i r n) -> p i r n", i=2, r=2)[:, :, r, :]

            for two in range(2):
                for r in range(2):
                    dve.wait_ge(*m["c_lg"].next())
                    for t in (2 * two, 2 * two + 1):
                        at = 256 * (t % 2)
                        V.tensor_tensor(parity(L, t, r),
                                        ps[:, 2 * two + r, at:at + 256].rearrange("p (i n) -> p i n", i=2),
                                        parity(bcs, t, r), ADD).then_inc(*m["tile_free"].tick())
            b.t = 0

            def heads(x):
                return x.rearrange("p (k n) -> p k n", n=32)

            def spread(at):
                return small[:, at:at + H2].unsqueeze(2).to_broadcast([P, H2, 32])

            for t in range(TT):
                dve.wait_ge(*m["tile_free"].upto(4 * (t // 2) - 5 + t % 2))
                V.tensor_reduce(small[:, 96 + 16 * t:112 + 16 * t], heads(L[:, t, :]), AX.X, MAX).then_inc(*m["c_mx"].tick())
            for t in range(TT):
                dve.wait_ge(*m["c_mx"].upto(t - 3))
                V.tensor_tensor(heads(L[:, t, :]), heads(L[:, t, :]), spread(96 + 16 * t), SUB).then_inc(*m["c_sub"].tick())
            for c in range(2 * GR):
                lower(HL[:, c, :], K32[:, c, :], HH[:, c, :], m["krep_hi"], m["krep_lo"])
            for t in range(TT):
                dve.wait_ge(*m["c_exp"].next())
                V.tensor_reduce(small[:, 160 + 16 * t:176 + 16 * t], heads(L[:, t, :]), AX.X, ADD).then_inc(*m["c_sum"].tick())
            dve.wait_ge(*m["c_sum"].upto())
            V.reciprocal(small[:, 160:224], small[:, 160:224]).then_inc(*m["c_inv"].tick())
            dve.wait_ge(*m["c_inv"].upto())
            dve.wait_ge(*m["gate_ok"].upto())
            for t in range(TT):
                gate = GT[:, t, :].rearrange("p (g i k) -> p i g k", g=GR, k=3)[:, :, :, 0]
                inv = small[:, 160 + 16 * t:176 + 16 * t].rearrange("p (i g) -> p i g", i=HG)
                V.tensor_tensor(inv, inv, gate, MUL).then_inc(*m["c_inv"].tick())
            for t in range(TT):
                dve.wait_ge(*m["c_inv"].upto(t - 3))
                V.tensor_tensor(heads(L[:, t, :]), heads(L[:, t, :]), spread(160 + 16 * t), MUL).then_inc(*m["c_mul"].tick())
            dve.wait_ge(*m["c_tr"].next(TT))
            NJ = 2 * H2
            for n in range(NJ + 1):
                if n < NJ:
                    hd = n // 2
                    if n % 2 == 0:
                        dve.wait_ge(strip_in[hd % 3], 16 * (hd // 3 + 1))
                    logits(n, JOBS2[n])
                if n >= 1:
                    normalise(n - 1, JOBS2[n - 1])
                if n >= 8 and n % 4 == 0:
                    c = (n - 8) // 4
                    lower(XL[:, c, :], O2[:, c, :], XH[:, c, :], m["x_hi"], m["x_lo"])
            lower(XL[:, 7, :], O2[:, 7, :], XH[:, 7, :], m["x_hi"], m["x_lo"])
            m["t_done"].next(3 * NJ)
            residual(4, 2, 2, "norm_mlp_1")
            mlp(None)
            invert(rstd[:, :])
            dve.wait_ge(*m["norm_inv"].upto())
            for c in range(DC):
                V.scalar_tensor_tensor(h[:, c, :], h[:, c, :], col("final_norm", c), rstd[:, :], MUL, MUL)\
                 .then_inc(*m["out_ok"].tick())


def blocks(w, nu, nt, cols):
    w = w[:, cols]
    n, k = w.shape[1], w.shape[0] // (nu * P)
    assert n == nt * P or nt == 0
    out = np.zeros((nu, P, 1024), w.dtype)
    out[:, :, :k * n] = w.reshape(nu, k, P, n).transpose(0, 2, 1, 3).reshape(nu, P, k * n)
    return out


def kernel(**inputs):
    import concourse.bacc as _bacc
    from concourse.bass_utils import run_bass_kernel_spmd as _run

    a = {k: np.asarray(v) for k, v in inputs.items()}
    R = np.arange
    w = []
    wi = a["w_in"][0]
    wi = np.concatenate([wi, np.zeros((D, 64), wi.dtype)], 1)
    o3 = QR + KVR + ROPE
    pair = R(256)
    kr = QR + KVR + R(ROPE)
    zero = o3 + 2 * CC + R(64)
    rot = np.concatenate([zero, kr, kr[16:], kr[:16]])
    for cols in (o3 + pair, o3 + CC + pair, pair, np.concatenate([256 + R(P), rot]), o3 + 256 + pair,
                 QR + pair, o3 + CC + 256 + pair):
        w.append(blocks(wi, 2, 2, cols))
    q = a["w_q_b"][0]
    head = [np.concatenate([96 * i + R(96), 96 * i + 80 + R(16), 96 * i + 64 + R(16)]) for i in range(H1)]
    for i in range(0, H1, 2):
        w.append(blocks(q, 1, 2, np.concatenate(head[i:i + 2])))
    kv = a["w_kv_b"][0]
    w.append(blocks(kv, 1, 4, np.concatenate([128 * i + R(64) for i in range(H1)])))
    w.append(blocks(kv, 1, 0, np.concatenate([128 * i + 64 + R(64) for i in range(H1)])))

    def full(m, nu=2):
        for i in range(m.shape[1] // 256):
            w.append(blocks(m, nu, 2, 256 * i + pair))

    full(a["w_o"][0])
    for i in range(2):
        w.append(blocks(a["w_ple_proj"][0], 1, 4, 512 * i + R(512)))
    g, u, dn = a["w_ffn_gate"][0], a["w_ffn_up"][0], a["w_ffn_down"][0]

    def ffn_up(grp, pairs):
        for i in range(pairs):
            w.append(blocks(g, 2, 2, 512 * grp + 256 * i + pair))
            w.append(blocks(u, 2, 2, 512 * grp + 256 * i + pair))

    def down(m, grp):
        full(m[512 * grp:512 * grp + 512], 1)

    ffn_up(0, 2)
    for i in range(1, 5):
        ffn_up(i, 2)
        down(dn, i - 1)
    ffn_up(5, 1)
    down(dn, 4)
    for i in range(2):
        w.append(blocks(dn[2560:], 1, 4, 512 * i + R(512)))
    full(a["w_ple_gate"][0])
    ai = a["a_w_in_2"][0]
    for i in range(4):
        for part in (1, 2, 0):
            w.append(blocks(ai, 2, 2, D * part + 256 * i + pair))
    full(a["a_w_out_2"][0])

    def mlp(layer):
        w1, w2 = a["mlp_w1_2"][layer], a["mlp_w2_2"][layer]
        for i in range(9):
            if i < 8:
                full(w1[:, 512 * i:512 * i + 512])
            if i:
                down(w2, i - 1)

    mlp(0)
    full(a["w_kv_2"])
    for n in ("phi_k_w1_2", "phi_v_w1_2"):
        w.append(blocks(a[n], 4, 2, pair))
    full(a["b_w_qg_2"][0][:, :D])
    w.append(blocks(a["b_w_qg_2"][0], 1, 0, D + R(48)))
    full(a["b_w_o_2"][0])
    mlp(1)
    weights = np.concatenate(w)
    assert weights.shape[0] == NU, (weights.shape, NU)

    def cols(v):
        v = np.asarray(v, np.float32).reshape(-1, P)
        return v.T

    lane = np.arange(P)
    inv = (10000.0 ** (-np.arange(0, ROPE, 2, dtype=np.float64) / ROPE)).astype(np.float32)
    vals = dict(
        g_mix_pre=a["g_mix_pre"], g_q_a=a["g_q_a"], g_kv_a=a["g_kv_a"], conv_b=a["conv_b"], conv_ln_g=a["conv_ln_g"],
        conv_ln_b=a["conv_ln_b"], g_mix_post=a["g_mix_post"], g_ffn_pre=a["g_ffn_pre"], ffn_dw_b=a["ffn_dw_b"],
        g_ffn_post=a["g_ffn_post"], g_ple=a["g_ple"], norm_mix_0=a["norm_mix_2"][0], norm_mix_1=a["norm_mix_2"][1],
        norm_mlp_0=a["norm_mlp_2"][0], norm_mlp_1=a["norm_mlp_2"][1], kv_norm=a["kv_norm_2"],
        final_norm=a["final_norm_2"], conv_w=a["conv_w"], ffn_dw_w=a["ffn_dw_w"], a_conv_w=a["a_conv_w_2"],
        freq=np.tile(inv, 8), cosine=np.where(lane < 96, 0.25, 0.0), quarter=np.where(lane < 96, np.pi / 2, 0.0),
        sign=np.where((lane >= 96) & (lane < 112), -1.0, 1.0), has_any=(lane >= 31).astype(np.float32), pe_k=a["cmp_pe_k_2"],
        pe_v=a["cmp_pe_v_2"])
    vecs = np.concatenate([cols(vals[n]) for n, _ in VECS], 1)
    assert vecs.shape == (P, NV)
    key, query = np.arange(S)[None, :] - (S - P), np.arange(P)[:, None]
    mask = np.where(key <= query, 0.0, NEG).astype(np.float32)

    def one_hot(dist):
        d = np.maximum(dist, 0)
        large = 16 + (np.log(np.maximum(d, 1) / 16.0) / math.log(8.0) * 16 + 1e-9).astype(np.int32)
        bucket = np.where(dist < 0, 32, np.where(d < 16, d, np.minimum(large, 31)))
        return (np.arange(33)[:, None] == bucket[None, :]).astype(np.float32)

    onehots = np.concatenate([one_hot(511 - R(640)), one_hot(R(1040) - 527)], 1)
    rb = np.concatenate([a["rel_bias_2"], np.full((1, H2), NEG, np.float32)])
    relb = np.concatenate([rb, rb[:, (R(HG)[:, None] + HG * R(GR)[None, :]).ravel()]], 1)

    def by_chunk(w):
        return w.reshape(2, P, HD).transpose(1, 0, 2)

    k2, v2 = by_chunk(a["phi_k_w2_2"]), by_chunk(a["phi_v_w2_2"])
    w2 = np.concatenate([np.concatenate([k2, k2], 2).reshape(P, 256), v2.reshape(P, P)], 1)

    ins = dict(onehots=onehots, relb=relb, w2=w2, xT=a["x"][0].T, pT=a["p"][0, 0].T, positions=a["positions"], weights=weights, vecs=vecs,
               mask=mask, ident=np.eye(P, dtype=np.float32))
    nc = _bacc.Bacc("TRN2", target_bir_lowering=False, num_devices=1)
    io, arrays = {}, {}
    for name, v in ins.items():
        arrays["in_" + name] = np.ascontiguousarray(v)
        io[name] = nc.dram_tensor("in_" + name, v.shape, mybir.dt.from_np(v.dtype), kind="ExternalInput").ap()
    io["tab"] = nc.dram_tensor("tab", (H2, P, 640), mybir.dt.float32, kind="Internal").ap()
    io["out"] = nc.dram_tensor("out_T", (D, S), mybir.dt.float32, kind="ExternalOutput").ap()
    build(nc, io)
    r = _run(nc, [arrays], core_ids=[0])
    return r.results[0]["out_T"].T.reshape(1, S, D)
```

```python
import math
from contextlib import ExitStack

import numpy as np
import concourse.bass as bass
from concourse import mybir

S, D, P = 512, 1024, 128
DC, TT = D // P, S // P
H1, NOPE, ROPE, VD = 8, 64, 32, 64
QR, KVR = 384, 256
CC, CW = 512, 31
FC = 22
H2, GR, HD = 16, 4, 64
HG = H2 // GR
EPS = 1e-6
NEG = -1e30
NSLOT = 4
SC1 = float(NOPE + ROPE) ** -0.5
SC2 = float(HD) ** -0.5

VECS = [("g_mix_pre", 8), ("g_q_a", 3), ("g_kv_a", 2), ("conv_b", 4), ("conv_ln_g", 4), ("conv_ln_b", 4),
        ("g_mix_post", 8), ("g_ffn_pre", 8), ("ffn_dw_b", 22), ("g_ffn_post", 8), ("g_ple", 8),
        ("norm_mix_0", 8), ("norm_mix_1", 8), ("norm_mlp_0", 8), ("norm_mlp_1", 8), ("kv_norm", 8),
        ("final_norm", 8), ("conv_w", CW * 4), ("ffn_dw_w", 3 * FC), ("a_conv_w", 3 * DC),
        ("freq", 1), ("cosine", 1), ("quarter", 1), ("sign", 1), ("has_any", 1), ("pe_k", 16), ("pe_v", 16)]
VO, NV = {}, 0
for _name, _n in VECS:
    VO[_name] = NV
    NV += _n

UNITS = [("in_proj", 14), ("q_b", 4), ("kv_b", 2), ("o", 8), ("ple", 2), ("ffn", 66), ("ple_gate", 8),
         ("a_in", 24), ("a_out", 8), ("mlp0", 64), ("kv", 12), ("phi", 8), ("q2", 8), ("gates", 1),
         ("o2", 8), ("mlp1", 64)]
NU = sum(n for _, n in UNITS)

UO, _at = {}, 0
for _name, _n in UNITS:
    UO[_name] = _at
    _at += _n
TURN = (6.28125, float(np.float32(0.0019350051879882812)), float(np.float32(2 * math.pi - 6.28125 - 0.0019350051879882812)))


SEMS = """
whi wlo used tile_done tile_free x_hi x_lo sq_done acc_add norm_sum norm_std norm_inv h_upd mask_in ident_in
vec_in rope_in p_in onehot_in relb_in w2_in const_ok ang ang_r2 rope_sin gt_sig c_ok qkv_g qkv_hi qkv_lo kr_part
kr_rope kr_copy qt_nope qt_r qt_rope q_hi q_lo k_half k_hi k_lo taps conv_xc conv_xn conv_act s_done l_done
neg_max p_exp p_inv p_norm t_done pt_act o_done o_out y_out y_tmp e_g ffn_t ffn_g ffn_gelu ffn_u hid_s hid_hi
hid_lo r_ok v_ok y_ok cu_t tab_done tab_out tab_st bc_in col_done col_ok kv_ok kr_ok kr_pad kr_hi kr_lo silu_ok
cmp_done kc_hi kc_lo vc_ok gate_s gate_ok c_lg c_mx lt_ok c_exp c_sum c_inv c_mul c_tr c_pt krep_hi krep_lo
ple_s out_ok out_st""".split()


class Mark:

    def __init__(self, sem, state):
        self.sem, self.state, self.n, self.step = sem, state, 0, 0

    def upto(self, k=0):
        v = self.n + k
        return (self.sem, v + self.step * self.state.i) if self.step else (self.sem, v)

    def tick(self):
        self.n += 1
        return self.sem, 1

    def next(self, k=1):
        self.n += k
        return self.upto()


class Turn:

    def __init__(self):
        self.i = 0


class Job:

    def __init__(self, qh, ql, kh, kl, v, p, pt, out, bias, scale, gate):
        self.qh, self.ql, self.kh, self.kl, self.v, self.p, self.pt = qh, ql, kh, kl, v, p, pt
        self.out, self.bias, self.scale, self.gate = out, bias, scale, gate


class Book:

    def __init__(self, sems):
        self.state = Turn()
        self.m = {k: Mark(v, self.state) for k, v in sems.items()}
        self.u = self.du = 0
        self.t = 0
        self.ahead = 0

    def turns(self, eng, count, du, steps):
        return _turns(self, eng, count, du, steps)


def _turns(book, eng, count, du, steps):
    from contextlib import contextmanager

    @contextmanager
    def run():
        n0 = {k: v.n for k, v in book.m.items()}
        u0, t0, a0 = book.u, book.t, book.ahead
        for k, v in steps.items():
            book.m[k].step = v
        book.du = du
        with eng.Fori(0, count) as i:
            book.state.i = i
            yield i
        book.state.i, book.du = 0, 0
        for k, v in book.m.items():
            got = v.n - n0[k]
            assert got == steps.get(k, 0), (k, got, steps.get(k, 0))
            v.n, v.step = n0[k] + got * count, 0
        assert book.u - u0 == du and book.ahead - a0 in (0, du) and (book.t - t0) % 4 == 0
        book.t = t0 + (book.t - t0) * count
        book.u = u0 + du * count
        book.ahead = a0 + (book.ahead - a0) * count
    return run()


def build(nc, io):
    f32, f32r = mybir.dt.float32, mybir.dt.float32r
    ACT, ALU, AX = mybir.ActivationFunctionType, mybir.AluOpType, mybir.AxisListType
    MUL, ADD, SUB, MAX = ALU.mult, ALU.add, ALU.subtract, ALU.max
    with ExitStack() as ctx:
        def sb(name, shape, dt=f32):
            return ctx.enter_context(nc.sbuf_tensor(name, shape, dt))

        raw = sb("raw", [P, NSLOT, 1024])
        WH = sb("WH", [P, NSLOT, 1024], f32r)
        WL = sb("WL", [P, NSLOT, 1024], f32r)
        XH = sb("XH", [P, DC, S], f32r)
        XL = sb("XL", [P, DC, S], f32r)
        HH = sb("HH", [P, DC, S], f32r)
        HL = sb("HL", [P, DC, S], f32r)
        h = sb("h", [P, DC, S])
        rstd = sb("rstd", [P, S])
        acc = sb("acc", [P, S])
        sq = sb("sq", [P, 2, S])
        vec = sb("vec", [P, NV])
        ident = sb("ident", [P, P])
        ones = sb("ones", [P, P])
        small = sb("small", [P, 256])
        ARENA = 16384
        ar = sb("arena", [P, ARENA])
        ps = ctx.enter_context(nc.psum_tensor("ps", [P, 8, S], f32))
        place = [0]

        def cut(n, at=None):
            if at is not None:
                place[0] = at
            a = place[0]
            place[0] += n
            assert place[0] <= ARENA, (place[0], ARENA)
            return ar[:, a:a + n]

        def cut(start, *shape):
            n = int(np.prod(shape))
            assert start + n <= ARENA, (start, n)
            v = ar[:, start:start + n]
            return v.rearrange("p (a b) -> p a b", a=shape[0]) if len(shape) == 2 else v

        PADW = S + CW - 1
        cpad = cut(0, 4, PADW)
        cacc = cut(2168, 4, S)
        V1 = cut(4216, TT, S)
        khat = cut(6264, H1, S)
        O1 = cut(6264, 4, S)
        mask1 = cut(10360, S)
        qkv = cut(10872, 5, S)
        gt = cut(13432, 2, S)
        rope = cut(14456, S)
        qt = cut(14968, 2, S)
        PB1 = [cut(x, 1280) for x in (10872, 12152, 8312)]
        PT1 = cut(13432, 2, 1280)
        Y = cut(0, DC, S)
        ple = cut(4096, DC, S)
        gpad = cut(8192, 2, S + 2)
        gc_ = cut(9232, 2, S)
        up = cut(10256, 2, S)
        ftmp = cut(11280, 2, S)
        ptmp = cut(12304, 2, S)
        xp = cut(13328, 2, S)

        rr, acs, apad = cut(0, S), cut(512, 2, S), cut(1536, 2, S + 2)
        act_, abs_, ay = cut(2564, 2, S), cut(3588, 2, S), cut(4612, 2, S)
        ohs, relb, tabs, bcs = cut(12304, 1680), cut(13984, H2), cut(5636, 1680), cut(9728, GR, S)
        rt, st_ = cut(0, 4, S), cut(2048, 4, S)
        K32, V2 = cut(0, 2 * GR, S), cut(4096, TT, S)
        KR = [cut(6600 + 1320 * i, 5, 264) for i in range(2)]
        FH = [XH[:, :, :].rearrange("p a b -> p (a b)")[:, 1320 * i:1320 * i + 1320].rearrange("p (g n) -> p g n", g=5)
              for i in range(2)]
        FL = [XL[:, :, :].rearrange("p a b -> p (a b)")[:, 1320 * i:1320 * i + 1320].rearrange("p (g n) -> p g n", g=5)
              for i in range(2)]
        w2s, hid, VC, GT, pre = cut(14848, 384), cut(15232, 2, P), sq[:, 0, 0:GR * HD], cut(16192, TT, 48), cut(15744, 2, 160)
        hidv = cut(12288, 2, GR * P)
        qst, L, PCT, LT = cut(6144, TT, S), cut(12288, TT, S), cut(6144, GR, S), cut(6144, GR, S)
        strips, PB2, PT2, O2 = cut(8192, 3, S), cut(9728, 3, 1280), cut(13568, 2, 1280), cut(0, DC, S)

        NMX, SUM, INV, MXC = 16, 32, 48, 64
        POFF = (0, 128, 384, 768)
        SCORES = ((0, 0, 0), (1, 0, P), (2, 1, 0), (3, 2, 0))
        TRANSPOSES = (tuple((0, q, q * P) for q in range(4)),
                      tuple((1, q, (q - 1) * P) for q in range(1, 4)) + ((3, 3, 3 * P),),
                      tuple((2, q, (q - 2) * P) for q in range(2, 4)))
        TBANK = (4, 5, 7)
        VALUES = (((0, 0),), ((1, 512), (3, 896)), ((2, 1024),))

        def LAST_OF_BANK(n, bk):
            k, g = divmod(3 * n + bk - 4, 3)
            return 4 * k + g + 2

        def job1(n):
            pair, r = divmod(n, 2)
            return Job(
                qh=XH[0:96, n, :], ql=XL[0:96, n, :], kh=HH[0:96, n, :], kl=HL[0:96, n, :],
                v=lambda kt: V1[:, kt, n * VD:(n + 1) * VD], p=lambda k: PB1[k % 3], pt=lambda k: PT1[:, k % 2, :],
                out=ps[64 * r:64 * r + 64, 6, :], bias=mask1, scale=SC1, gate=None)

        def job2(n):
            hd, br = divmod(n, 2)
            pair, r = divmod(hd, 2)
            g = hd // HG
            x = slice(64 * r, 64 * r + 64)
            return Job(
                qh=XH[x, pair, :], ql=XL[x, pair, :], kh=HH[x, br * GR + g, :], kl=HL[x, br * GR + g, :],
                v=lambda kt: V2[:, kt, br * 256 + HD * g:br * 256 + HD * g + HD], p=lambda k: PB2[:, k % 3, :],
                pt=lambda k: PT2[:, k % 2, :], out=ps[x, 6, :], bias=strips[:, hd % 3, :], scale=1.0,
                gate=GT[:, :, 3 * hd + 1 + br])

        KEYS = [4 * br + g for g in range(GR) for br in range(2)]
        JOBS2 = [job2(n) for n in range(2 * H2)]
        JOBS1 = [job1(n) for n in range(H1)]

        strip_in = [ctx.enter_context(nc.semaphore(f"strip_in{s}")) for s in range(3)]
        KCH = sb("KCH", [P, GR * 64], f32r)
        KCL = sb("KCL", [P, GR * 64], f32r)

        def of_head(x, r):
            return x[64 * r:64 * r + 64, :].rearrange("p (g r n) -> p g r n", g=GR, r=2)[:, :, r, :]

        def of_group(x, r):
            return x[64 * r:64 * r + 64].rearrange("p (g n) -> p g n", g=GR)

        sems = {name: ctx.enter_context(nc.semaphore(name)) for name in SEMS}
        x_in = [ctx.enter_context(nc.semaphore(f"x_in{c}")) for c in range(DC)]
        raw_in = [ctx.enter_context(nc.semaphore(f"raw_in{s}")) for s in range(NSLOT)]

        def col(name, c=0):
            return vec[:, VO[name] + c:VO[name] + c + 1]

        def raw_ready(b, k):
            u = b.u + k if not isinstance(k, tuple) else k[0]
            return raw_in[u % NSLOT], 16 * (u // NSLOT + 1) + (16 * (b.du // NSLOT) * b.state.i if b.du else 0)

        def units(b, n, k=0):
            return n + k + (b.du * b.state.i if b.du else 0)

        block = ctx.enter_context(nc.Block())

        @block.sync
        def _(sp):
            for c in range(DC):
                if c % 2 == 0:
                    sp.dma_start(raw[:, c // 2, :], io["weights"][c // 2]).then_inc(raw_in[c // 2], 16)
                sp.dma_start(h[:, c, :], io["xT"][c * P:(c + 1) * P, :]).then_inc(x_in[c], 16)

            def weights(a, b):
                full = (b - a) // NSLOT
                if full:
                    with sp.Fori(0, full) as i:
                        for k in range(NSLOT):
                            sp.wait_ge(sems["wlo"], NSLOT * i + a + k - NSLOT + 1)
                            sp.dma_start(raw[:, (a + k) % NSLOT, :], io["weights"][NSLOT * i + (a + k)])\
                              .then_inc(raw_in[(a + k) % NSLOT], 16)
                for u in range(a + full * NSLOT, b):
                    sp.wait_ge(sems["wlo"], u - NSLOT + 1)
                    sp.dma_start(raw[:, u % NSLOT, :], io["weights"][u]).then_inc(raw_in[u % NSLOT], 16)

            weights(NSLOT, UO["o2"] + NSLOT)
            sp.wait_ge(sems["tab_st"], 32)
            for hd in range(H2):
                if hd < 3:
                    sp.wait_ge(sems["kr_lo"], 2)
                else:
                    sp.wait_ge(sems["l_done"], 4 * H1 + 8 * (hd - 2))
                sp.dma_start(strips[:, hd % 3, :], bass.AP(io["tab"].tensor, hd * 640 * P + 127, [[639, P], [1, S]]))\
                  .then_inc(strip_in[hd % 3], 16)
            weights(UO["o2"] + NSLOT, NU)
            for c in range(DC):
                sp.wait_ge(sems["out_ok"], c + 1)
                sp.dma_start(io["out"][c * P:(c + 1) * P, :], h[:, c, :]).then_inc(sems["out_st"], 16)
            sp.wait_ge(sems["out_st"], 16 * DC)

        @block.gpsimd
        def _(pool):
            nc.gpsimd.memset(ones[:, :], 1.0).then_inc(sems["const_ok"], 1)
            nc.gpsimd.memset(cpad[:, :, 0:CW - 1], 0.0).then_inc(sems["const_ok"], 1)

            def lower(u, s):
                pool.wait_ge(sems["whi"], u + 1)
                nc.gpsimd.tensor_tensor(WL[:, s, :], raw[:, s, :], WH[:, s, :].bitcast(f32), SUB)\
                  .then_inc(sems["wlo"], 1)

            def lower_heads(out, src, up_, hi, lo, heads):
                for hd in heads:
                    pool.wait_ge(sems[hi], hd + 1)
                    nc.gpsimd.tensor_tensor(out[0:96, hd, :], src(hd), up_[0:96, hd, :].bitcast(f32), SUB)\
                      .then_inc(sems[lo], 1)

            with pool.Fori(0, 4) as i:
                for k in range(NSLOT):
                    lower(NSLOT * i + k, k)
            for j in range(4):
                lower(16 + j, j)
                lower_heads(XL, lambda hd: qt[0:96, hd % 2, :], XH, "q_hi", "q_lo", (2 * j, 2 * j + 1))
            for u in range(20, 24):
                lower(u, u % NSLOT)
            lower_heads(HL, lambda hd: khat[0:96, hd, :], HH, "k_hi", "k_lo", range(H1))
            with pool.Fori(0, NU // NSLOT - 6) as i:
                for k in range(NSLOT):
                    lower(NSLOT * i + (24 + k), k)
            for u in range(NU // NSLOT * NSLOT, NU):
                lower(u, u % NSLOT)

        @block.tensor
        def _(pe):
            b = Book(sems)
            m = b.m

            def three(out, wh, wl, xh, xl, start, stop):
                nc.tensor.matmul(out, wh, xh, start=start, stop=False)
                nc.tensor.matmul(out, wh, xl, start=False, stop=False)
                return nc.tensor.matmul(out, wl, xh, start=False, stop=stop)

            def project(nu, nk, nt, xh, xl, x_sem=None, cols=lambda x, c: x[:, c, :], n=S, part=None):
                first, end = part or (0, nu)
                for j in range(first, end):
                    pe.wait_ge(sems["wlo"], units(b, b.u, j - first + 1))
                    s = (b.u + j - first) % NSLOT
                    for t in range(nt):
                        if j == 0 and b.t + t >= 4:
                            pe.wait_ge(*m["tile_free"].upto(t - 3))
                        for k in range(nk):
                            c = j * nk + k
                            if t == 0 and x_sem is not None:
                                pe.wait_ge(*x_sem.upto(c + 1))
                            w = slice(k * nt * P + t * P, k * nt * P + (t + 1) * P)
                            last = three(ps[:, (b.t + t) % 4, 0:n], WH[:, s, w], WL[:, s, w], cols(xh, c), cols(xl, c),
                                         c == 0, c == nu * nk - 1)
                        if t == nt - 1:
                            last.then_inc(*m["used"].tick())
                        elif j == nu - 1:
                            last.then_inc(*m["tile_done"].tick())
                b.u += end - first
                if end == nu:
                    b.t += nt
                    m["tile_free"].n += nt

            def by_token(nu, nk, n, xh, xl):
                for j in range(nu):
                    pe.wait_ge(sems["wlo"], units(b, b.u, j + 1))
                    s = (b.u + j) % NSLOT
                    for t in range(TT):
                        if j == 0:
                            pe.wait_ge(*m["tile_free"].upto(t - 3))
                        for k in range(nk):
                            c = j * nk + k
                            x = slice(t * P, (t + 1) * P)
                            last = three(ps[:, (b.t + t) % 4, 0:n], xh[:, c, x], xl[:, c, x],
                                         WH[:, s, k * n:(k + 1) * n], WL[:, s, k * n:(k + 1) * n],
                                         c == 0, c == nu * nk - 1)
                        if t == TT - 1:
                            last.then_inc(*m["used"].tick())
                        elif j == nu - 1:
                            last.then_inc(*m["tile_done"].tick())
                b.u += nu
                b.t += TT
                m["tile_free"].n += TT

            def total(n, bank=7):
                pe.wait_ge(*m["acc_add"].next(n))
                nc.tensor.matmul(ps[:, bank, :], ones[:, :], acc[:, :], start=True, stop=True)\
                  .then_inc(*m["norm_sum"].tick())

            def scores(n, job):
                for qs, bk, at in SCORES:
                    bank = (3 * n + bk) % 4
                    if at == 0:
                        if (3 * n + bk) >= 4:
                            pe.wait_ge(*m["l_done"].upto(LAST_OF_BANK(n, bk)))
                        else:
                            pe.wait_ge(*m["tile_free"].upto())
                    w = P * (qs + 1)
                    q = slice(qs * P, w)
                    last = three(ps[:, bank, at:at + w], job.qh[:, q], job.ql[:, q], job.kh[:, 0:w], job.kl[:, 0:w],
                                 True, True)
                    if qs:
                        last.then_inc(*m["s_done"].tick())

            def transposes(n, job):
                m["p_norm"].next(4)
                pe.wait_ge(*m["p_norm"].upto())
                for g, group in enumerate(TRANSPOSES):
                    c = 3 * n + g
                    if c >= 3:
                        pe.wait_ge(*m["pt_act"].upto(c - 2))
                    for kt, qs, at in group:
                        last = nc.tensor.transpose(ps[:, TBANK[g], at:at + P],
                                                   job.p(n)[:, POFF[qs] + kt * P:POFF[qs] + (kt + 1) * P], ident[:, :])
                    last.then_inc(*m["t_done"].tick())

            def values(n, job, first, last):
                for g, kts in enumerate(VALUES):
                    pe.wait_ge(*m["pt_act"].upto(3 * n + g + 1))
                    for kt, at in kts:
                        done = nc.tensor.matmul(job.out[:, kt * P:S], job.v(kt), job.pt(n)[:, at:at + S - kt * P],
                                                start=first and kt == 0, stop=last and (g, kt) == (2, 2),
                                                skip_group_check=True)
                done.then_inc(*m["o_done"].tick())

            def tables():
                pe.wait_ge(sems["onehot_in"], 16)
                pe.wait_ge(sems["relb_in"], 16)
                for k in range(0, 1680, S):
                    if k >= 2 * S:
                        pe.wait_ge(*m["tab_out"].upto(k // S - 1))
                    w = min(S, 1680 - k)
                    nc.tensor.matmul(ps[0:H2, 4 + k // S % 2, 0:w], relb[0:33, 0:H2], ohs[0:33, k:k + w],
                                     start=True, stop=True).then_inc(*m["tab_done"].tick())
                m["tab_out"].next(4)

            pe.wait_ge(sems["const_ok"], 2)

            pe.wait_ge(sems["vec_in"], 16)
            project(2, 4, 2, XH, XL, m["x_lo"])
            total(7)
            m["x_lo"].next(DC)
            for _ in range(4):
                project(2, 4, 2, XH, XL)
            total(2)
            for _ in range(2):
                project(2, 4, 2, XH, XL)
            total(1)
            for j in range(4):
                project(1, 3, 2, HH, HL, m["qkv_lo"] if j == 0 else None)
            m["qkv_lo"].next(3)
            project(1, 2, 4, HH[:, 3:5, :], HL[:, 3:5, :], m["qkv_lo"])
            m["qkv_lo"].next(2)
            by_token(1, 2, S, HH[:, 3:5, :], HL[:, 3:5, :])

            pe.wait_ge(sems["ident_in"], 16)
            for n in range(H1 + 3):
                if n < H1:
                    pe.wait_ge(*m["q_lo"].upto(n + 1))
                    pe.wait_ge(*m["k_lo"].upto(n + 1))
                    scores(n, JOBS1[n])
                if n >= 3:
                    k = n - 3
                    if k % 2 == 0 and k >= 2:
                        pe.wait_ge(*m["o_out"].upto(k // 2))
                    values(k, JOBS1[k], True, True)
                if 2 <= n <= H1 + 1:
                    transposes(n - 2, JOBS1[n - 2])
            m["l_done"].next(4 * H1)
            m["pt_act"].next(3 * H1)
            m["o_out"].next(H1 // 2)
            m["q_lo"].next(H1)
            m["k_lo"].next(H1)

            project(4, 2, 4, XH, XL, m["x_lo"], part=(0, 2))
            total(3)
            pe.wait_ge(*m["conv_xc"].next(4))
            total(3)
            project(4, 2, 4, XH, XL, m["x_lo"], part=(2, 4))
            project(4, 2, 4, XH, XL)
            m["x_lo"].next(DC)
            total(7)

            for j in range(2):
                project(1, 2, 4, HH, HL, m["hid_lo"] if j == 0 else None)
            m["hid_lo"].next(2)
            total(7)

            def ffn_up(pairs, x_sem=None):
                for j in range(pairs):
                    project(2, 4, 2, XH, XL, x_sem if j == 0 else None)
                    if j == 0 and x_sem is not None:
                        x_sem.next(DC)
                        total(7)
                    project(2, 4, 2, XH, XL)

            def down(par, last=False):
                pe.wait_ge(*m["hid_lo"].next(2 if last else 4))
                if last:
                    for _ in range(2):
                        project(1, 2, 4, HH[:, par * 4:par * 4 + 2, :], HL[:, par * 4:par * 4 + 2, :])
                else:
                    for _ in range(4):
                        project(1, 4, 2, HH[:, par * 4:par * 4 + 4, :], HL[:, par * 4:par * 4 + 4, :])

            ffn_up(2, m["x_lo"])
            with b.turns(pe, 2, 24, dict(used=24, tile_done=16, tile_free=32, hid_lo=8)):
                for par in range(2):
                    ffn_up(2)
                    down(par)
            ffn_up(1)
            down(0)
            down(1, True)
            total(7)

            for j in range(2):
                project(4, 2, 4, XH, XL, m["x_lo"] if j == 0 else None)
            m["x_lo"].next(DC)

            for j in range(4):
                project(2, 4, 2, HH, HL, m["x_lo"] if j == 0 else None)
                if j == 0:
                    m["x_lo"].next(DC)
                    total(7)
                project(2, 4, 2, HH, HL)
                project(2, 4, 2, HH, HL)
                if j == 1:
                    tables()
            for j in range(2):
                project(4, 2, 4, XH, XL, m["x_lo"] if j == 0 else None)
            m["x_lo"].next(DC)

            def mlp():
                def up_(par, x_sem=None):
                    project(2, 4, 2, HH, HL, x_sem)
                    if x_sem is not None:
                        x_sem.next(DC)
                        total(7)
                    project(2, 4, 2, HH, HL)

                def down_(par):
                    pe.wait_ge(*m["hid_lo"].next(4))
                    for _ in range(4):
                        project(1, 4, 2, XH[:, par * 4:par * 4 + 4, :], XL[:, par * 4:par * 4 + 4, :])

                up_(0, m["x_lo"])
                with b.turns(pe, 3, 16, dict(used=16, tile_done=12, tile_free=24, hid_lo=8)):
                    for par in range(2):
                        up_(1 - par)
                        down_(par)
                up_(1)
                down_(0)
                down_(1)

            mlp()

            for j in range(3):
                project(2, 4, 2, HH, HL, m["x_lo"] if j == 0 else None)
                if j == 0:
                    m["x_lo"].next(DC)
                    total(7)
                    project(2, 4, 2, HH, HL)
                    m["norm_inv"].n = m["norm_sum"].n - 1
                    pe.wait_ge(*m["norm_inv"].upto())
                    for t in range(TT):
                        last = nc.tensor.transpose(ps[:, 6, t * P:(t + 1) * P], rstd[:, t * P:(t + 1) * P], ident[:, :])
                    last.then_inc(*m["col_done"].tick())
                else:
                    by_token(2, 4, 256, HH, HL)
            for i in range(2):
                pe.wait_ge(*m["kr_lo"].next())
                project(4, 4, 2, FH[i], FL[i], cols=lambda x, c: x[:, :, c:c + 249:8], n=5 * 32)
            pe.wait_ge(*m["col_ok"].next())
            pe.wait_ge(sems["w2_in"], 16)
            for i in range(2):
                pe.wait_ge(*m["silu_ok"].next(2))
                if i == 0:
                    for c in range(2):
                        last = nc.tensor.matmul(ps[:, 6, 0:P], w2s[:, c * P:(c + 1) * P], hid[:, c, :],
                                                start=c == 0, stop=c == 1)
                else:
                    for g in range(GR):
                        for c in range(2):
                            last = nc.tensor.matmul(ps[:, 5, HD * g:HD * g + HD],
                                                    hidv[:, c, g * P:(g + 1) * P],
                                                    w2s[:, 256 + c * HD:256 + (c + 1) * HD], start=c == 0, stop=c == 1)
                last.then_inc(*m["cmp_done"].tick())
            for j in range(2):
                project(4, 2, 4, HH, HL, m["x_lo"] if j == 0 else None)
            m["x_lo"].next(DC)
            by_token(1, 8, 3 * H2, HH, HL)

            pe.wait_ge(*m["q_lo"].next(DC))
            pe.wait_ge(*m["kc_lo"].next(2))
            for c in range(DC):
                pe.wait_ge(*m["tile_free"].upto(c - 3))
                w = slice(64 * (c // 2), 64 * (c // 2) + 64)
                three(ps[0:64, (b.t + c) % 4, :], KCH[:, w], KCL[:, w], XH[:, c, :], XL[:, c, :], True, True)\
                    .then_inc(*m["c_lg"].tick())
            m["tile_free"].n += DC
            b.t = 0
            pe.wait_ge(*m["lt_ok"].next(GR))
            for t in range(TT):
                for g in range(GR):
                    last = nc.tensor.transpose(ps[:, t, g * P:(g + 1) * P], LT[:, g, t * P:(t + 1) * P], ident[:, :])
                last.then_inc(*m["c_lg"].tick())
            m["tile_free"].n += TT

            def compressed_transposes():
                for t in range(TT):
                    pe.wait_ge(*m["c_mul"].next())
                    if t >= 2:
                        pe.wait_ge(*m["c_pt"].upto(t - 1))
                    if t < 2:
                        pe.wait_ge(*m["vc_ok"].upto(1))
                    for g in range(GR):
                        last = nc.tensor.transpose(ps[:, 4 + t % 2, g * P:(g + 1) * P], L[:, t, g * P:(g + 1) * P],
                                                   ident[:, :])
                    last.then_inc(*m["c_tr"].tick())
                pe.wait_ge(*m["c_pt"].next(TT))

            NJ = 2 * H2
            for n in range(NJ + 3):
                if n < NJ:
                    if n % (2 * HG) == 0:
                        pe.wait_ge(*m["krep_lo"].next(2))
                    scores(n, JOBS2[n])
                if n == 0:
                    compressed_transposes()
                if n >= 3:
                    k = n - 3
                    if k % 4 == 0 and k >= 4:
                        pe.wait_ge(*m["o_out"].upto(k // 4))
                    if k == 0:
                        pe.wait_ge(*m["kc_lo"].upto())
                    if k % 2 == 0:
                        g, i = divmod(k // 2, HG)
                        nc.tensor.matmul(JOBS2[k].out, VC[32 * i:32 * i + 32, HD * g:HD * g + HD],
                                         PCT[32 * i:32 * i + 32, g, :],
                                         start=True, stop=False, skip_group_check=True)
                    values(k, JOBS2[k], False, k % 2 == 1)
                if 2 <= n <= NJ + 1:
                    transposes(n - 2, JOBS2[n - 2])
            m["l_done"].next(4 * NJ)
            m["pt_act"].next(3 * NJ)
            m["o_out"].next(DC)
            for j in range(2):
                project(4, 2, 4, XH, XL, m["x_lo"] if j == 0 else None)
            m["x_lo"].next(DC)
            mlp()
            total(7)

        @block.scalar
        def _(act):
            b = Book(sems)
            m = b.m

            def upper(upto):
                while b.ahead < min(upto, NU):
                    u, s, i = b.ahead, b.ahead % NSLOT, b.du * b.state.i if b.du else 0
                    act.wait_ge(raw_in[s], 16 * (u // NSLOT + 1) + (16 * (b.du // NSLOT) * b.state.i if b.du else 0))
                    if u >= NSLOT:
                        act.wait_ge(sems["used"], u - NSLOT + 1 + i)
                    nc.scalar.activation(WH[:, s, :], raw[:, s, :], ACT.Copy).then_inc(*m["whi"].tick())
                    b.ahead += 1

            def landed(nu, nt, j):
                return (sems["used"], units(b, b.u, nu)) if j == nt - 1 else m["tile_done"].upto(j + 1)

            def close(nu, nt):
                b.u += nu
                b.t += nt
                m["tile_done"].n += nt - 1
                m["tile_free"].n += nt

            def square(c, src, n):
                if c == 0:
                    if m["norm_sum"].n:
                        act.wait_ge(*m["norm_sum"].upto())
                    nc.scalar.activation(acc[:, :], src, ACT.Square).then_inc(*m["sq_done"].tick())
                else:
                    if m["acc_add"].n >= 2:
                        act.wait_ge(*m["acc_add"].upto(-1))
                    nc.scalar.activation(sq[:, m["acc_add"].n % 2, :], src, ACT.Square).then_inc(*m["sq_done"].tick())
                    m["acc_add"].next()

            def root(out, n):
                act.wait_ge(*m["norm_sum"].next())
                nc.scalar.activation(out, ps[:, 7, :], ACT.Sqrt, bias=small[:, 0:1], scale=1.0 / n)\
                  .then_inc(*m["norm_std"].tick())

            def split_h(gain, src_sem=None):
                for c in range(DC):
                    if src_sem is not None:
                        act.wait_ge(*src_sem.next())
                    else:
                        if c % 2 == 0:
                            upper(c // 2 + 1)
                        act.wait_ge(x_in[c], 16)
                    if c == 0 and b.u:
                        act.wait_ge(sems["used"], b.u)
                    nc.scalar.activation(XH[:, c, :], h[:, c, :], ACT.Copy, scale=col(gain, c)).then_inc(*m["x_hi"].tick())
                    square(c, h[:, c, :], DC)

            act.dma_start(vec[:, :], io["vecs"]).then_inc(sems["vec_in"], 16)
            act.dma_start(qt[64:128, 1, :].bitcast(mybir.dt.int32), io["positions"].to_broadcast([64, S]))\
               .then_inc(sems["rope_in"], 16)
            act.dma_start(mask1, io["mask"]).then_inc(sems["mask_in"], 16)
            act.dma_start(ident[:, :], io["ident"]).then_inc(sems["ident_in"], 16)
            act.wait_ge(sems["vec_in"], 16)
            split_h("g_mix_pre")
            root(rstd[:, :], D)

            act.wait_ge(*m["ang_r2"].next())
            nc.scalar.activation(rope[64:128, :], gt[64:128, 1, :], ACT.Sin).then_inc(*m["rope_sin"].tick())

            def gates():
                for j in range(2):
                    act.wait_ge(*m["tile_free"].upto(j + 1))
                    nc.scalar.activation(gt[:, j, :], gt[:, j, :], ACT.Sigmoid).then_inc(*m["gt_sig"].tick())
                close(2, 2)

            upper(b.u + 4)
            close(2, 2)
            upper(b.u + 4)
            gates()
            upper(b.u + 4)
            for j in range(2):
                act.wait_ge(*m["tile_free"].upto(j + 1))
                square(j, qkv[:, j, :], 3)
            close(2, 2)
            upper(b.u + 4)
            act.wait_ge(*m["tile_free"].upto(1))
            square(2, qkv[:, 2, :], 3)
            close(2, 2)
            upper(b.u + 4)
            close(2, 2)
            root(V1[:, 0, :], QR)
            upper(b.u + 4)
            for j in range(2):
                act.wait_ge(*m["tile_free"].upto(j + 1))
                square(j, qkv[:, 3 + j, :], 2)
            close(2, 2)
            for c in range(3):
                act.wait_ge(*m["qkv_g"].next())
                nc.scalar.activation(HH[:, c, :], qkv[:, c, :], ACT.Copy).then_inc(*m["qkv_hi"].tick())
            upper(b.u + 4)
            gates()
            upper(b.u + 3)
            root(V1[:, 1, :], KVR)
            for c in range(3, 5):
                act.wait_ge(*m["qkv_g"].next())
                nc.scalar.activation(HH[:, c, :], qkv[:, c, :], ACT.Copy).then_inc(*m["qkv_hi"].tick())
            act.wait_ge(*m["kr_rope"].next())
            for hd in range(1, H1):
                nc.scalar.activation(khat[64:96, hd, :], khat[64:96, 0, :], ACT.Copy).then_inc(*m["kr_copy"].tick())

            for j in range(4):
                upper(b.u + 3)
                for t in range(2):
                    hd = 2 * j + t
                    act.wait_ge(*landed(1, 2, t))
                    if hd >= 2:
                        act.wait_ge(*m["q_lo"].upto(hd - 1))
                    nc.scalar.activation(qt[0:64, hd % 2, :], ps[0:64, (b.t + t) % 4, :], ACT.Copy)\
                      .then_inc(*m["qt_nope"].tick())
                    act.wait_ge(*m["qt_rope"].next())
                    nc.scalar.activation(XH[0:96, hd, :], qt[0:96, hd % 2, :], ACT.Copy).then_inc(*m["q_hi"].tick())
                close(1, 2)
            m["q_lo"].next(H1)
            upper(b.u + 4)
            for t in range(4):
                act.wait_ge(*landed(1, 4, t))
                nc.scalar.activation(khat[0:64, 2 * t, :], ps[0:64, (b.t + t) % 4, :], ACT.Copy).then_inc(*m["k_half"].tick())
            close(1, 4)
            close(1, 4)
            upper(b.u + 4)
            act.wait_ge(sems["used"], b.u)
            act.wait_ge(*m["kr_copy"].upto())
            for hd in range(H1):
                act.wait_ge(*m["tile_free"].upto(-8 + hd // 2 + 1))
                nc.scalar.activation(HH[0:96, hd, :], khat[0:96, hd, :], ACT.Copy).then_inc(*m["k_hi"].tick())

            def exponentials(n, job, scale):
                act.wait_ge(*m["neg_max"].next())
                for qs in range(TT):
                    a = job.p(n)[:, POFF[qs]:POFF[qs] + P * (qs + 1)]
                    k = 8 * (n % 2) + qs
                    nc.scalar.activation(a, a, ACT.Exp, bias=small[:, NMX + k:NMX + k + 1], scale=scale,
                                         accum_out=small[:, SUM + k:SUM + k + 1]).then_inc(*m["p_exp"].tick())

            def copy_transposed(n, job):
                for g, (at, w) in enumerate(((0, 512), (512, 512), (1024, 256))):
                    act.wait_ge(*m["t_done"].next())
                    if g == 0 and n >= 2:
                        act.wait_ge(*m["o_done"].upto(n - 1))
                    nc.scalar.activation(job.pt(n)[:, at:at + w], ps[:, TBANK[g], 0:w], ACT.Copy)\
                      .then_inc(*m["pt_act"].tick())

            def head_pair_out(pair, out):
                act.wait_ge(*m["o_done"].upto(2 * pair + 2))
                nc.scalar.activation(out, ps[:, 6, :], ACT.Copy).then_inc(*m["o_out"].tick())

            act.wait_ge(*m["k_lo"].next(H1))
            for n in range(H1 + 2):
                if n >= 2:
                    copy_transposed(n - 2, JOBS1[n - 2])
                if n >= 4 and n % 2 == 0:
                    head_pair_out((n - 4) // 2, O1[:, (n - 4) // 2, :])
                if n < H1:
                    exponentials(n, JOBS1[n], SC1)
            head_pair_out(3, O1[:, 3, :])
            m["o_done"].next(H1)

            act.dma_start(xp, io["pT"].rearrange("(c p) n -> p c n", p=P)).then_inc(sems["p_in"], 16)
            act.wait_ge(*m["s_done"].next(3 * H1))
            for c in range(4):
                act.wait_ge(*m["o_out"].upto(c - 3))
                nc.scalar.activation(XH[:, c, :], O1[:, c, :], ACT.Copy).then_inc(*m["x_hi"].tick())
            m["conv_xc"].next(4)
            m["acc_add"].next(3)
            m["norm_sum"].next()
            for c in range(4):
                act.wait_ge(*m["conv_xc"].upto(c - 3))
                square(c, cacc[:, c, :], CC)
            root(rstd[:, :], CC)
            for c in range(4):
                act.wait_ge(*m["conv_xn"].next())
                nc.scalar.activation(cacc[:, c, :], cacc[:, c, :], ACT.Silu, bias=col("conv_ln_b", c),
                                     scale=col("conv_ln_g", c)).then_inc(*m["conv_act"].tick())
            for c in range(4):
                act.wait_ge(*m["conv_act"].upto(c - 3))
                nc.scalar.activation(XH[:, 4 + c, :], cacc[:, c, :], ACT.Copy).then_inc(*m["x_hi"].tick())
            for j in range(2):
                upper(b.u + 4)
                upper(b.u + 7)
                for t in range(4):
                    act.wait_ge(*m["tile_free"].upto(t + 1))
                    square(4 * j + t, Y[:, 4 * j + t, :], D)
                close(4, 4)
            upper(b.u + 3)
            root(rstd[:, :], D)

            act.wait_ge(sems["p_in"], 16)
            for c in range(2):
                nc.scalar.activation(HH[:, c, :], xp[:, c, :], ACT.Copy).then_inc(*m["hid_hi"].tick())
            for j in range(2):
                upper(b.u + 3)
                for t in range(4):
                    act.wait_ge(*m["tile_free"].upto(t + 1))
                    square(4 * j + t, ple[:, 4 * j + t, :], D)
                close(1, 4)
            root(up[:, 0, :], D)
            upper(b.u + 4)
            split_h("g_ffn_pre", m["h_upd"])
            root(rstd[:, :], D)

            def ffn_up(pairs, par):
                for pr in range(pairs):
                    upper(b.u + 4)
                    upper(b.u + 6)
                    for j in range(2):
                        act.wait_ge(*m["ffn_g"].next())
                        nc.scalar.activation(gc_[:, j, :], gc_[:, j, :], ACT.Gelu_apprx_tanh).then_inc(*m["ffn_gelu"].tick())
                    close(2, 2)
                    upper(b.u + 4)
                    for j in range(2):
                        act.wait_ge(*m["hid_s"].next())
                        nc.scalar.activation(HH[:, 4 * par + 2 * pr + j, :], ftmp[:, j, :], ACT.Copy)\
                          .then_inc(*m["hid_hi"].tick())
                    close(2, 2)

            def down_rest(n, nt):
                for _ in range(n):
                    upper(b.u + 3)
                    close(1, nt)

            ffn_up(2, 0)
            upper(b.u + 3)
            lead = b.ahead - b.u
            with b.turns(act, 2, 24, dict(whi=24, tile_done=16, tile_free=32, ffn_g=8, ffn_gelu=8, hid_s=8, hid_hi=8)):
                for par in range(2):
                    ffn_up(2, 1 - par)
                    down_rest(4, 2)
                upper(b.u + lead)
            ffn_up(1, 1)
            down_rest(4, 2)
            for j in range(2):
                upper(b.u + 3)
                for t in range(4):
                    act.wait_ge(*m["tile_free"].upto(t + 1))
                    square(4 * j + t, Y[:, 4 * j + t, :], D)
                close(1, 4)
            root(rstd[:, :], D)

            for c in range(DC):
                if c == 1:
                    upper(b.u + 4)
                act.wait_ge(*m["h_upd"].next())
                nc.scalar.activation(XH[:, c, :], h[:, c, :], ACT.Copy).then_inc(*m["x_hi"].tick())

            def split_chunk(gain, c):
                if gain is not None:
                    nc.scalar.activation(HH[:, c, :], h[:, c, :], ACT.Copy, scale=col(gain, c)).then_inc(*m["x_hi"].tick())
                square(c, h[:, c, :], DC)

            for j in range(3):
                if j < 2:
                    upper(b.u + 4)
                    upper(b.u + 7)
                    for t in range(4):
                        act.wait_ge(*landed(4, 4, t))
                        nc.scalar.activation(ps[:, (b.t + t) % 4, :], ps[:, (b.t + t) % 4, :], ACT.Sigmoid)\
                          .then_inc(*m["ple_s"].tick())
                    close(4, 4)
                if j >= 1:
                    for t in range(4):
                        act.wait_ge(*m["h_upd"].next())
                        split_chunk("norm_mix_0", 4 * j - 4 + t)
            upper(b.u + 4)
            root(rstd[:, :], D)
            act.dma_start(ohs[0:33, :], io["onehots"]).then_inc(sems["onehot_in"], 16)
            act.dma_start(relb[0:33, :], io["relb"]).then_inc(sems["relb_in"], 16)
            act.dma_start(w2s, io["w2"]).then_inc(sems["w2_in"], 16)

            for j in range(4):
                upper(b.u + 4)
                close(2, 2)
                upper(b.u + 4)
                close(2, 2)
                upper(b.u + 4)
                for t in range(2):
                    act.wait_ge(*m["y_ok"].next())
                    nc.scalar.activation(XH[:, 2 * j + t, :], ay[:, t, :], ACT.Copy).then_inc(*m["x_hi"].tick())
                close(2, 2)
                if j == 1:
                    act.wait_ge(*m["tab_out"].next(4))
                    act.dma_start(io["ftab"], tabs[0:H2, 640:].unsqueeze(1).to_broadcast([H2, 32, 1040]))\
                       .then_inc(sems["tab_st"], 16)
                    act.dma_start(io["tab"], tabs[0:H2, 0:640].unsqueeze(1).to_broadcast([H2, P, 640]))\
                       .then_inc(sems["tab_st"], 16)

            def residual(n, nu, nt, gain):
                for j in range(n):
                    upper(b.u + (3 if nu == 1 else 4))
                    if nu == 4:
                        upper(b.u + 7)
                    for t in range(nt):
                        act.wait_ge(*m["tile_free"].upto(t + 1))
                        split_chunk(gain, nt * j + t)
                    close(nu, nt)

            residual(2, 4, 4, "norm_mlp_0")
            act.wait_ge(sems["tab_st"], 32)
            for g in range(GR):
                act.dma_start(bcs[:, g, :], bass.AP(io["ftab"].tensor, HG * g * 32 * 1040 + 496,
                                                    [[32 * 1040, HG], [1040 - 16, 32], [1, S]])).then_inc(sems["bc_in"], 16)

            def mlp(gain):
                upper(b.u + 4)
                root(rstd[:, :], D)

                def up_(par):
                    for pr in range(2):
                        upper(b.u + 4)
                        for t in range(2):
                            act.wait_ge(*m["tile_free"].upto(t + 1))
                            nc.scalar.activation(XH[:, 4 * par + 2 * pr + t, :], rt[:, 2 * pr + t, :], ACT.Square)\
                              .then_inc(*m["hid_hi"].tick())
                        close(2, 2)

                up_(0)
                upper(b.u + 3)
                lead = b.ahead - b.u
                with b.turns(act, 3, 16, dict(whi=16, tile_done=12, tile_free=24, hid_hi=8)):
                    for par in range(2):
                        up_(1 - par)
                        down_rest(4, 2)
                    upper(b.u + lead)
                up_(1)
                down_rest(4, 2)
                residual(4, 1, 2, gain)

            mlp("kv_norm")

            upper(b.u + 4)
            root(rstd[:, :], D)
            upper(b.u + 4)
            close(2, 2)
            upper(b.u + 4)
            close(2, 2)
            for i in range(2):
                act.wait_ge(*m["kr_pad"].next(10))
                nc.scalar.activation(FH[i], KR[i], ACT.Copy).then_inc(*m["kr_hi"].tick())
            for _ in range(2):
                upper(b.u + 4)
                close(2, 2)
                upper(b.u + 4)
                close(2, 4)
            act.wait_ge(sems["used"], b.u)
            for i in range(2):
                upper(b.u + 4)
                if i == 0:
                    for c in range(DC):
                        nc.scalar.activation(HH[:, c, :], h[:, c, :], ACT.Copy, scale=col("norm_mix_1", c))\
                          .then_inc(*m["x_hi"].tick())
                for t in range(2):
                    act.wait_ge(*m["tile_free"].upto(t + 1))
                    if i == 0:
                        out, src = hid[:, t, :], pre[:, t, 0:P]
                    else:
                        out = hidv[:, t, :].rearrange("p (g i n) -> p g i n", g=GR, i=HG)
                        src = pre[:, t, 0:P].rearrange("p (g n) -> p g n", g=GR).unsqueeze(2)\
                            .to_broadcast([P, GR, HG, 32])
                    nc.scalar.activation(out, src, ACT.Silu, bias=pre[:, t, P:P + 1]).then_inc(*m["silu_ok"].tick())
                close(4, 2)
            upper(b.u + 4)
            act.wait_ge(*m["cmp_done"].next())
            act.wait_ge(*m["kr_ok"].next(4))
            for r in range(2):
                nc.scalar.activation(of_head(KCH, r), of_group(ps[:, 6, 0:P], r), ACT.Copy).then_inc(*m["kc_hi"].tick())
            for j in range(2):
                upper(b.u + 4)
                upper(b.u + 7)
                for t in range(4):
                    act.wait_ge(*m["tile_free"].upto(t + 1))
                    nc.scalar.activation(XH[:, 4 * j + t, :], qst[:, t, :], ACT.Copy).then_inc(*m["q_hi"].tick())
                close(4, 4)
            upper(b.u + 3)
            act.wait_ge(*m["tile_free"].upto(4))
            nc.scalar.activation(GT, GT, ACT.Sigmoid).then_inc(*m["gate_s"].tick())
            close(1, 4)
            m["tile_free"].n += DC + TT
            b.t = 0
            act.wait_ge(*m["kv_ok"].next(16))
            for c in KEYS:
                nc.scalar.activation(HH[:, c, :], K32[:, c, :], ACT.Copy).then_inc(*m["krep_hi"].tick())
            upper(b.u + 4)
            for t in range(TT):
                act.wait_ge(*m["tile_free"].upto(t - 3))
                nc.scalar.activation(L[:, t, :], L[:, t, :], ACT.Exp).then_inc(*m["c_exp"].tick())
            for t in range(TT):
                act.wait_ge(*m["c_tr"].next())
                nc.scalar.activation(PCT[:, :, t * P:(t + 1) * P],
                                     ps[:, 4 + t % 2, :].rearrange("p (g q) -> p g q", g=GR), ACT.Copy)\
                  .then_inc(*m["c_pt"].tick())
            act.wait_ge(*m["krep_lo"].next(2 * GR))

            def pair_out(pair):
                act.wait_ge(*m["o_done"].upto(4 * pair + 4))
                nc.scalar.activation(O2[:, pair, :], ps[:, 6, :], ACT.Copy).then_inc(*m["o_out"].tick())
                act.wait_ge(*m["o_out"].upto())
                nc.scalar.activation(XH[:, pair, :], O2[:, pair, :], ACT.Copy).then_inc(*m["x_hi"].tick())

            NJ = 2 * H2
            for n in range(NJ + 2):
                if n >= 2:
                    copy_transposed(n - 2, JOBS2[n - 2])
                if n >= 6 and n % 4 == 2:
                    pair_out((n - 6) // 4)
                if n < NJ:
                    exponentials(n, JOBS2[n], 1.0)
            pair_out(DC - 1)
            m["o_done"].next(NJ)
            residual(2, 4, 4, "norm_mlp_1")
            mlp(None)
            root(rstd[:, :], D)

        @block.vector
        def _(dve):
            b = Book(sems)
            m = b.m
            V = nc.vector

            def landed(nu, nt, j):
                return (sems["used"], units(b, b.u, nu)) if j == nt - 1 else m["tile_done"].upto(j + 1)

            def bank(j, n=S):
                return ps[:, (b.t + j) % 4, 0:n]

            def close(nu, nt):
                b.u += nu
                b.t += nt
                m["tile_done"].n += nt - 1

            def add_square(c):
                m["sq_done"].next()
                if c:
                    dve.wait_ge(*m["sq_done"].upto())
                    if c > 1:
                        dve.wait_ge(*m["acc_add"].upto())
                    V.tensor_tensor(acc[:, :], acc[:, :], sq[:, m["acc_add"].n % 2, :], ADD).then_inc(*m["acc_add"].tick())

            def invert(x):
                m["norm_sum"].next()
                dve.wait_ge(*m["norm_std"].next())
                V.reciprocal(x, x).then_inc(*m["norm_inv"].tick())

            def lower_h(gain, c):
                dve.wait_ge(*m["x_hi"].next())
                V.scalar_tensor_tensor(XL[:, c, :], h[:, c, :], col(gain, c), XH[:, c, :].bitcast(f32), MUL, SUB)\
                 .then_inc(*m["x_lo"].tick())

            def lower(out, src, up_, hi, lo):
                dve.wait_ge(*hi.next())
                V.tensor_tensor(out, src, up_.bitcast(f32), SUB).then_inc(*lo.tick())

            V.memset(small[:, :], EPS).then_inc(*m["taps"].tick())
            dve.wait_ge(sems["vec_in"], 16)
            for c in range(DC):
                lower_h("g_mix_pre", c)
                add_square(c)
            dve.wait_ge(sems["rope_in"], 16)
            lanes = slice(64, 128)
            ang, red, whole = gt[lanes, 0, :], gt[lanes, 1, :], qt[lanes, 0, :]
            V.tensor_copy(ang, qt[lanes, 1, :].bitcast(mybir.dt.int32)).then_inc(*m["ang"].tick())
            dve.wait_ge(*m["ang"].upto())
            V.tensor_scalar(ang, ang, vec[lanes, VO["freq"]:VO["freq"] + 1], None, MUL).then_inc(*m["ang"].tick())
            dve.wait_ge(*m["ang"].upto())
            V.tensor_scalar(red, ang, 1 / (2 * math.pi), vec[lanes, VO["cosine"]:VO["cosine"] + 1], MUL, ADD)\
             .then_inc(*m["ang"].tick())
            dve.wait_ge(*m["ang"].upto())
            V.tensor_copy(whole.bitcast(mybir.dt.int32), red).then_inc(*m["ang"].tick())
            dve.wait_ge(*m["ang"].upto())
            V.tensor_copy(whole, whole.bitcast(mybir.dt.int32)).then_inc(*m["ang"].tick())
            for n, part in enumerate(TURN):
                dve.wait_ge(*m["ang"].upto())
                V.scalar_tensor_tensor(red, whole, -part, ang if n == 0 else red, MUL, ADD).then_inc(*m["ang"].tick())
            dve.wait_ge(*m["ang"].upto())
            V.tensor_scalar(red, red, vec[lanes, VO["quarter"]:VO["quarter"] + 1], None, ADD).then_inc(*m["ang"].tick())
            dve.wait_ge(*m["ang"].upto())
            V.tensor_scalar(red, red, 3.1415925, -3.1415925, ALU.min, MAX).then_inc(*m["ang_r2"].tick())

            invert(rstd[:, :])
            dve.wait_ge(*m["rope_sin"].next())
            V.tensor_scalar(rope[lanes, :], rope[lanes, :], vec[lanes, VO["sign"]:VO["sign"] + 1], None, MUL)\
             .then_inc(*m["ang"].tick())

            def taps():
                for first in (0, 2):
                    for k in range(CW):
                        for c in (first, first + 1):
                            yield k, c

            steps = taps()
            base = m["taps"].n

            def convolve(n):
                for _ in range(n):
                    k, c = next(steps, (None, None))
                    if k is None:
                        return
                    if k:
                        dve.wait_ge(*m["taps"].upto(-1))
                    w = vec[:, VO["conv_w"] + 4 * k + c:VO["conv_w"] + 4 * k + c + 1]
                    if k == 0:
                        V.tensor_scalar(cacc[:, c, :], cpad[:, c, 0:S], w, col("conv_b", c), MUL, ADD)\
                         .then_inc(*m["taps"].tick())
                    else:
                        V.scalar_tensor_tensor(cacc[:, c, :], cpad[:, c, k:k + S], w, cacc[:, c, :], MUL, ADD)\
                         .then_inc(*m["taps"].tick())

            def channels(c0):
                for j in range(2):
                    dve.wait_ge(*landed(2, 2, j))
                    V.tensor_tensor(cpad[:, c0 + j, CW - 1:PADW], bank(j), rstd[:, :], MUL).then_inc(*m["tile_free"].tick())
                close(2, 2)

            def gates(c0):
                for j in range(2):
                    dve.wait_ge(*landed(2, 2, j))
                    V.tensor_tensor(gt[:, j, :], bank(j), rstd[:, :], MUL).then_inc(*m["tile_free"].tick())
                close(2, 2)
                for j in range(2):
                    dve.wait_ge(*m["gt_sig"].next())
                    V.tensor_tensor(cpad[:, c0 + j, CW - 1:PADW], cpad[:, c0 + j, CW - 1:PADW], gt[:, j, :], MUL)\
                     .then_inc(*m["c_ok"].tick())
                dve.wait_ge(*m["c_ok"].upto())

            def low_rank(c, j):
                dve.wait_ge(*landed(2, 2, j))
                V.tensor_tensor(qkv[:, c, :], bank(j), rstd[:, :], MUL).then_inc(*m["tile_free"].tick())

            def normalised(c, gain, k, root_):
                V.scalar_tensor_tensor(qkv[:, c, :], qkv[:, c, :], col(gain, k), root_, MUL, MUL).then_inc(*m["qkv_g"].tick())

            dve.wait_ge(*m["norm_inv"].upto())
            dve.wait_ge(sems["const_ok"], 2)
            channels(0)
            gates(0)
            for j in range(2):
                low_rank(j, j)
                add_square(j)
            close(2, 2)
            convolve(8)
            low_rank(2, 0)
            add_square(2)
            dve.wait_ge(*landed(2, 2, 1))
            V.tensor_tensor(qt[lanes, 1, :], ps[lanes, (b.t + 1) % 4, :], rstd[lanes, :], MUL).then_inc(*m["tile_free"].tick())
            dve.wait_ge(*m["tile_free"].upto())
            dve.wait_ge(*m["ang"].upto())
            V.tensor_tensor(qt[64:96, 0, :], qt[96:128, 1, :], rope[96:128, :], MUL).then_inc(*m["kr_part"].tick())
            V.tensor_tensor(khat[64:96, 0, :], qt[64:96, 1, :], rope[64:96, :], MUL).then_inc(*m["kr_part"].tick())
            dve.wait_ge(*m["kr_part"].upto())
            V.tensor_tensor(khat[64:96, 0, :], khat[64:96, 0, :], qt[64:96, 0, :], ADD).then_inc(*m["kr_rope"].tick())
            close(2, 2)
            convolve(10)
            channels(2)
            convolve(8)
            invert(V1[:, 0, :])
            dve.wait_ge(*m["norm_inv"].upto())
            for c in range(3):
                normalised(c, "g_q_a", c, V1[:, 0, :])
            for j in range(2):
                low_rank(3 + j, j)
                add_square(j)
            close(2, 2)
            for c in range(3):
                lower(HL[:, c, :], qkv[:, c, :], HH[:, c, :], m["qkv_hi"], m["qkv_lo"])
            convolve(10)
            gates(2)
            invert(V1[:, 1, :])
            dve.wait_ge(*m["norm_inv"].upto())
            for c in range(3, 5):
                normalised(c, "g_kv_a", c - 3, V1[:, 1, :])
            for c in range(3, 5):
                lower(HL[:, c, :], qkv[:, c, :], HH[:, c, :], m["qkv_hi"], m["qkv_lo"])

            for j in range(4):
                for t in range(2):
                    hd = 2 * j + t
                    dve.wait_ge(*landed(1, 2, t))
                    bk = ps[:, (b.t + t) % 4, :]
                    if hd >= 2:
                        dve.wait_ge(*m["q_lo"].upto(hd - 1))
                    V.tensor_tensor(qt[64:96, hd % 2, :], bk[96:128], rope[96:128, :], MUL).then_inc(*m["qt_r"].tick())
                    dve.wait_ge(*m["qt_nope"].next())
                    V.tensor_tensor(gt[64:96, hd % 2, :], bk[64:96], rope[64:96, :], MUL).then_inc(*m["tile_free"].tick())
                    dve.wait_ge(*m["qt_r"].upto())
                    dve.wait_ge(*m["tile_free"].upto())
                    V.tensor_tensor(qt[64:96, hd % 2, :], qt[64:96, hd % 2, :], gt[64:96, hd % 2, :], ADD)\
                     .then_inc(*m["qt_rope"].tick())
                    convolve(2)
                close(1, 2)
            m["q_hi"].next(H1)
            m["q_lo"].next(H1)
            for t in range(4):
                dve.wait_ge(*landed(1, 4, t))
                dve.wait_ge(*m["k_half"].next())
                V.tensor_copy(khat[0:64, 2 * t + 1, :], ps[64:128, (b.t + t) % 4, :]).then_inc(*m["tile_free"].tick())
            close(1, 4)
            for t in range(4):
                dve.wait_ge(*landed(1, 4, t))
                V.tensor_copy(V1[:, t, :], bank(t)).then_inc(*m["tile_free"].tick())
            close(1, 4)
            m["k_hi"].next(H1)
            m["k_lo"].next(H1)

            def logits(n, job):
                if n == 2:
                    dve.wait_ge(*m["k_lo"].upto())
                if n >= 3:
                    dve.wait_ge(*m["t_done"].upto(3 * (n - 2)))
                for qs, bk, at in SCORES:
                    w = P * (qs + 1)
                    k = 8 * (n % 2) + qs
                    dve.wait_ge(*(m["s_done"].upto() if qs == 1 else m["s_done"].next()))
                    V.tensor_tensor_reduce(out=job.p(n)[:, POFF[qs]:POFF[qs] + w],
                                           in0=ps[:, (3 * n + bk) % 4, at:at + w], in1=job.bias[:, S - w:S], scale=1.0,
                                           scalar=-3.0e38, op0=ADD, op1=MAX,
                                           accum_out=small[:, MXC + k:MXC + k + 1]).then_inc(*m["l_done"].tick())
                k = 8 * (n % 2)
                dve.wait_ge(*m["l_done"].upto())
                V.tensor_scalar(small[:, NMX + k:NMX + k + 4], small[:, MXC + k:MXC + k + 4], -job.scale, None, MUL)\
                 .then_inc(*m["neg_max"].tick())

            def normalise(n, job):
                k = 8 * (n % 2)
                m["p_exp"].next(4)
                dve.wait_ge(*m["p_exp"].upto())
                V.reciprocal(small[:, INV + k:INV + k + 4], small[:, SUM + k:SUM + k + 4]).then_inc(*m["p_inv"].tick())
                if job.gate is not None:
                    dve.wait_ge(*m["p_inv"].upto())
                    V.tensor_tensor(small[:, INV + k:INV + k + 4], small[:, INV + k:INV + k + 4], job.gate, MUL)\
                     .then_inc(*m["p_inv"].tick())
                dve.wait_ge(*m["p_inv"].upto())
                for qs in range(TT):
                    a = job.p(n)[:, POFF[qs]:POFF[qs] + P * (qs + 1)]
                    V.tensor_scalar(a, a, small[:, INV + k + qs:INV + k + qs + 1], None, MUL).then_inc(*m["p_norm"].tick())

            dve.wait_ge(sems["mask_in"], 16)
            for n in range(H1 + 1):
                if n < H1:
                    logits(n, JOBS1[n])
                if n >= 1:
                    normalise(n - 1, JOBS1[n - 1])
                convolve(8)
            m["t_done"].next(3 * H1)

            for c in range(4):
                m["o_out"].next()
                lower(XL[:, c, :], O1[:, c, :], XH[:, c, :], m["x_hi"], m["x_lo"])
            convolve(4 * CW)
            dve.wait_ge(*m["taps"].upto())
            dve.wait_ge(*m["norm_sum"].upto())
            for c in range(1, 4):
                V.tensor_tensor(acc[:, :], cacc[:, 0, :] if c == 1 else acc[:, :], cacc[:, c, :], ADD)\
                 .then_inc(*m["acc_add"].tick())
                dve.wait_ge(*m["acc_add"].upto())
            dve.wait_ge(*m["norm_sum"].next())
            for c in range(4):
                V.scalar_tensor_tensor(cacc[:, c, :], ps[:, 7, :], -1.0 / CC, cacc[:, c, :], MUL, ADD)\
                 .then_inc(*m["conv_xc"].tick())
            for c in range(4):
                add_square(c)
            invert(rstd[:, :])
            dve.wait_ge(*m["norm_inv"].upto())
            for c in range(4):
                V.tensor_tensor(cacc[:, c, :], cacc[:, c, :], rstd[:, :], MUL).then_inc(*m["conv_xn"].tick())
            for c in range(4):
                lower(XL[:, 4 + c, :], cacc[:, c, :], XH[:, 4 + c, :], m["x_hi"], m["x_lo"])
            for j in range(2):
                for t in range(4):
                    dve.wait_ge(*landed(4, 4, t))
                    V.tensor_copy(Y[:, 4 * j + t, :], bank(t)).then_inc(*m["tile_free"].tick())
                    if t or j:
                        add_square(4 * j + t - 1)
                close(4, 4)
            add_square(DC - 1)

            def add_normalised(gain, c, src):
                V.scalar_tensor_tensor(src[:, c, :], src[:, c, :], col(gain, c), rstd[:, :], MUL, MUL).then_inc(*m["y_tmp"].tick())
                dve.wait_ge(*m["y_tmp"].upto())
                V.tensor_tensor(h[:, c, :], h[:, c, :], src[:, c, :], ADD).then_inc(*m["h_upd"].tick())

            dve.wait_ge(sems["p_in"], 16)
            for c in range(2):
                lower(HL[:, c, :], xp[:, c, :], HH[:, c, :], m["hid_hi"], m["hid_lo"])
            for j in range(2):
                for t in range(4):
                    dve.wait_ge(*landed(1, 4, t))
                    V.tensor_copy(ple[:, 4 * j + t, :], bank(t)).then_inc(*m["tile_free"].tick())
                    if t or j:
                        add_square(4 * j + t - 1)
                close(1, 4)
            add_square(DC - 1)
            invert(rstd[:, :])
            dve.wait_ge(*m["norm_inv"].upto())
            for c in range(DC):
                add_normalised("g_mix_post", c, Y)
                lower_h("g_ffn_pre", c)
                add_square(c)
            invert(up[:, 0, :])
            dve.wait_ge(*m["norm_inv"].upto())
            for c in range(DC):
                V.scalar_tensor_tensor(ple[:, c, :], ple[:, c, :], col("g_ple", c), up[:, 0, :], MUL, MUL)\
                 .then_inc(*m["e_g"].tick())
            for c in range(DC):
                V.memset(Y[:, c, :], 0.0).then_inc(*m["y_out"].tick())
            V.memset(gpad[:, :, 0:2], 0.0).then_inc(*m["y_out"].tick())
            invert(rstd[:, :])
            dve.wait_ge(*m["norm_inv"].upto())
            dve.wait_ge(*m["y_out"].upto())

            def dw(k, f):
                o = VO["ffn_dw_b"] if k == 3 else VO["ffn_dw_w"] + k * FC
                return vec[:, bass.ds(o + f, 1)] if not isinstance(f, int) else vec[:, o + f:o + f + 1]

            def ffn_up(f0, pairs, par):
                for pr in range(pairs):
                    f = [f0 + 2 * pr + j for j in range(2)]
                    for j in range(2):
                        dve.wait_ge(*landed(2, 2, j))
                        V.tensor_tensor(gpad[:, j, 2:S + 2], bank(j), rstd[:, :], MUL).then_inc(*m["tile_free"].tick())
                    close(2, 2)
                    dve.wait_ge(*m["tile_free"].upto())
                    for j in range(2):
                        V.tensor_scalar(gc_[:, j, :], gpad[:, j, 2:S + 2], dw(2, f[j]), dw(3, f[j]), MUL, ADD)\
                         .then_inc(*m["ffn_t"].tick())
                    for j in range(2):
                        dve.wait_ge(*m["ffn_t"].upto(j - 1))
                        V.scalar_tensor_tensor(gc_[:, j, :], gpad[:, j, 1:S + 1], dw(1, f[j]), gc_[:, j, :], MUL, ADD)\
                         .then_inc(*m["ffn_u"].tick())
                    for j in range(2):
                        dve.wait_ge(*m["ffn_u"].upto(j - 1))
                        V.scalar_tensor_tensor(gc_[:, j, :], gpad[:, j, 0:S], dw(0, f[j]), gc_[:, j, :], MUL, ADD)\
                         .then_inc(*m["ffn_g"].tick())
                    for j in range(2):
                        dve.wait_ge(*landed(2, 2, j))
                        V.tensor_tensor(up[:, j, :], bank(j), rstd[:, :], MUL).then_inc(*m["tile_free"].tick())
                    close(2, 2)
                    dve.wait_ge(*m["tile_free"].upto())
                    for j in range(2):
                        dve.wait_ge(*m["ffn_gelu"].next())
                        V.tensor_tensor(ftmp[:, j, :], gc_[:, j, :], up[:, j, :], MUL).then_inc(*m["hid_s"].tick())
                    for j in range(2):
                        s = 4 * par + 2 * pr + j
                        lower(HL[:, s, :], ftmp[:, j, :], HH[:, s, :], m["hid_hi"], m["hid_lo"])

            def add_downs(n, nt, squares=False):
                for j in range(n):
                    for t in range(nt):
                        dve.wait_ge(*landed(1, nt, t))
                        dve.wait_ge(*m["tile_free"].upto())
                        V.tensor_tensor(Y[:, nt * j + t, :], Y[:, nt * j + t, :], bank(t), ADD).then_inc(*m["tile_free"].tick())
                        if squares and (t or j):
                            add_square(nt * j + t - 1)
                    close(1, nt)
                if squares:
                    add_square(DC - 1)

            ffn_up(0, 2, 0)
            with b.turns(dve, 2, 24, dict(tile_done=16, tile_free=32, ffn_t=8, ffn_u=8, ffn_g=8, ffn_gelu=8, hid_s=8,
                                          hid_hi=8, hid_lo=8)) as i:
                for par in range(2):
                    ffn_up(8 * i + 4 + 4 * par, 2, 1 - par)
                    add_downs(4, 2)
            ffn_up(20, 1, 1)
            add_downs(4, 2)
            add_downs(2, 4, True)
            invert(rstd[:, :])
            dve.wait_ge(*m["norm_inv"].upto())
            for c in range(DC):
                add_normalised("g_ffn_post", c, Y)
                dve.wait_ge(*m["x_hi"].next())
                V.tensor_tensor(XL[:, c, :], h[:, c, :], XH[:, c, :].bitcast(f32), SUB).then_inc(*m["x_lo"].tick())

            def lower_chunk(gain, c):
                if gain is not None:
                    dve.wait_ge(*m["x_hi"].next())
                    V.scalar_tensor_tensor(HL[:, c, :], h[:, c, :], col(gain, c), HH[:, c, :].bitcast(f32), MUL, SUB)\
                     .then_inc(*m["x_lo"].tick())
                add_square(c)

            for j in range(3):
                if j < 2:
                    for t in range(4):
                        c = 4 * j + t
                        dve.wait_ge(*m["ple_s"].next())
                        dve.wait_ge(*m["h_upd"].upto(-1))
                        V.tensor_tensor(ptmp[:, t % 2, :], bank(t), ple[:, c, :], MUL).then_inc(*m["tile_free"].tick())
                        dve.wait_ge(*m["tile_free"].upto())
                        V.tensor_tensor(h[:, c, :], h[:, c, :], ptmp[:, t % 2, :], ADD).then_inc(*m["h_upd"].tick())
                    close(4, 4)
                    dve.wait_ge(*m["h_upd"].upto())
                if j >= 1:
                    for t in range(4):
                        lower_chunk("norm_mix_0", 4 * j - 4 + t)
            V.memset(apad[:, :, 0:2], 0.0).then_inc(*m["v_ok"].tick())
            invert(rstd[:, :])
            dve.wait_ge(*m["norm_inv"].upto())
            V.tensor_tensor(rr, rstd[:, :], rstd[:, :], MUL).then_inc(*m["r_ok"].tick())
            dve.wait_ge(*m["r_ok"].upto())

            def copy_tables():
                for k in range(0, 1680, S):
                    w = min(S, 1680 - k)
                    dve.wait_ge(*m["tab_done"].next())
                    V.tensor_copy(tabs[0:H2, k:k + w], ps[0:H2, 4 + k // S % 2, 0:w]).then_inc(*m["tab_out"].tick())

            for j in range(4):
                for t in range(2):
                    dve.wait_ge(*landed(2, 2, t))
                    V.tensor_tensor(acs[:, t, :], bank(t), rr, MUL).then_inc(*m["tile_free"].tick())
                close(2, 2)
                dve.wait_ge(*m["tile_free"].upto())
                if j:
                    dve.wait_ge(*m["cu_t"].upto())
                for t in range(2):
                    dve.wait_ge(*landed(2, 2, t))
                    V.tensor_tensor(apad[:, t, 2:S + 2], bank(t), acs[:, t, :], MUL).then_inc(*m["tile_free"].tick())
                close(2, 2)
                dve.wait_ge(*m["tile_free"].upto())
                dve.wait_ge(*m["v_ok"].upto())
                if j:
                    dve.wait_ge(*m["y_ok"].upto())
                for k in (2, 1, 0):
                    for t in range(2):
                        w = col("a_conv_w", k * DC + 2 * j + t)
                        if k == 2:
                            V.tensor_scalar(act_[:, t, :], apad[:, t, 2:S + 2], w, None, MUL).then_inc(*m["cu_t"].tick())
                        else:
                            dve.wait_ge(*m["cu_t"].upto(-1))
                            V.scalar_tensor_tensor(act_[:, t, :], apad[:, t, k:k + S], w, act_[:, t, :], MUL, ADD)\
                             .then_inc(*m["cu_t"].tick())
                dve.wait_ge(*m["cu_t"].upto())
                for t in range(2):
                    dve.wait_ge(*landed(2, 2, t))
                    V.tensor_tensor(abs_[:, t, :], bank(t), rstd[:, :], MUL).then_inc(*m["tile_free"].tick())
                close(2, 2)
                dve.wait_ge(*m["tile_free"].upto())
                if j:
                    dve.wait_ge(*m["x_lo"].upto())
                for t in range(2):
                    V.tensor_tensor(ay[:, t, :], act_[:, t, :], abs_[:, t, :], MUL).then_inc(*m["y_ok"].tick())
                for t in range(2):
                    lower(XL[:, 2 * j + t, :], ay[:, t, :], XH[:, 2 * j + t, :], m["x_hi"], m["x_lo"])
                if j == 1:
                    copy_tables()

            def residual(n, nu, nt, gain):
                for j in range(n):
                    for t in range(nt):
                        c = nt * j + t
                        dve.wait_ge(*landed(nu, nt, t))
                        V.tensor_tensor(h[:, c, :], h[:, c, :], bank(t), ADD).then_inc(*m["tile_free"].tick())
                        if c:
                            lower_chunk(gain, c - 1)
                    close(nu, nt)
                dve.wait_ge(*m["tile_free"].upto())
                lower_chunk(gain, nt * n - 1)

            residual(2, 4, 4, "norm_mlp_0")

            def mlp(gain):
                invert(rstd[:, :])
                dve.wait_ge(*m["norm_inv"].upto())
                dve.wait_ge(*m["x_lo"].upto())

                def up_(par):
                    for pr in range(2):
                        for t in range(2):
                            dve.wait_ge(*landed(2, 2, t))
                            V.scalar_tensor_tensor(rt[:, 2 * pr + t, :], bank(t), 0.0, rstd[:, :], MAX, MUL)\
                             .then_inc(*m["tile_free"].tick())
                        close(2, 2)
                        dve.wait_ge(*m["tile_free"].upto())
                        for t in range(2):
                            V.tensor_tensor(st_[:, 2 * pr + t, :], rt[:, 2 * pr + t, :], rt[:, 2 * pr + t, :], MUL)\
                             .then_inc(*m["hid_s"].tick())
                        dve.wait_ge(*m["hid_s"].upto())
                        for t in range(2):
                            c = 4 * par + 2 * pr + t
                            lower(XL[:, c, :], st_[:, 2 * pr + t, :], XH[:, c, :], m["hid_hi"], m["hid_lo"])

                def down_():
                    for j in range(4):
                        for t in range(2):
                            c = 2 * j + t
                            dve.wait_ge(*landed(1, 2, t))
                            V.tensor_tensor(h[:, c, :], h[:, c, :], bank(t), ADD).then_inc(*m["tile_free"].tick())
                        close(1, 2)
                    dve.wait_ge(*m["tile_free"].upto())
                    dve.wait_ge(*m["hid_lo"].upto())

                up_(0)
                dve.wait_ge(*m["hid_lo"].upto())
                with b.turns(dve, 3, 16, dict(tile_done=12, tile_free=24, hid_hi=8, hid_s=8, hid_lo=8)):
                    for par in range(2):
                        up_(1 - par)
                        down_()
                up_(1)
                down_()
                residual(4, 1, 2, gain)

            mlp("kv_norm")

            dve.wait_ge(sems["tab_st"], 32)
            for i in range(2):
                V.memset(KR[i], 0.0).then_inc(*m["kr_ok"].tick())
            dve.wait_ge(*m["kr_ok"].upto())
            for part in (KCH, KCL):
                V.tensor_copy(part[:, :], KR[0][:, 0, 0:GR * 64]).then_inc(*m["kr_ok"].tick())
            invert(rstd[:, :])
            dve.wait_ge(*m["norm_inv"].upto())
            dve.wait_ge(*m["kr_ok"].upto())
            dve.wait_ge(*m["hid_lo"].upto())
            for i, name in enumerate(("pe_k", "pe_v")):
                for t in range(2):
                    dve.wait_ge(*landed(2, 2, t))
                    for gi in range(2):
                        rows = slice(64 * gi, 64 * gi + 64)
                        for odd in range(2):
                            V.tensor_tensor(KR[i][64 * odd:64 * odd + 64, 2 * t + gi, 0:256],
                                            ps[rows, (b.t + t) % 4, odd::2], rstd[rows, odd::2], MUL)\
                             .then_inc(*m["kr_pad"].tick())
                    dve.wait_ge(*m["kr_pad"].upto())
                    V.tensor_copy(KR[i][:, 4, 8 * t:8 * t + 8], vec[:, VO[name] + 8 * t:VO[name] + 8 * t + 8])\
                     .then_inc(*m["kr_pad"].tick())
                    V.tensor_copy(small[:, 1:2], small[:, 0:1]).then_inc(*m["tile_free"].tick())
                close(2, 2)
            dve.wait_ge(*m["kr_pad"].upto())
            dve.wait_ge(*m["col_done"].next())
            V.tensor_copy(small[:, 80:84], ps[:, 6, 0:S:P]).then_inc(*m["col_ok"].tick())
            dve.wait_ge(*m["col_ok"].upto())
            for i in range(2):
                dve.wait_ge(*m["kr_hi"].next())
                V.tensor_tensor(FL[i], KR[i], FH[i].bitcast(f32), SUB).then_inc(*m["kr_lo"].tick())
            for br in range(2):
                for t in range(2):
                    dve.wait_ge(*landed(2, 2, t))
                    for gi in range(2):
                        rows = slice(64 * gi, 64 * gi + 64)
                        for half in range(2):
                            V.tensor_tensor(K32[64 * half:64 * half + 64, br * 4 + 2 * t + gi, :],
                                            ps[rows, (b.t + t) % 4, :], rstd[rows, :], MUL).then_inc(*m["kv_ok"].tick())
                    dve.wait_ge(*m["kv_ok"].upto())
                    V.tensor_copy(small[:, 1:2], small[:, 0:1]).then_inc(*m["tile_free"].tick())
                close(2, 2)
                for t in range(TT):
                    dve.wait_ge(*landed(2, 4, t))
                    V.tensor_scalar(V2[:, t, br * 256:br * 256 + 256], bank(t, 256), small[:, 80 + t:81 + t], None, MUL)\
                     .then_inc(*m["tile_free"].tick())
                close(2, 4)
            for i in range(2):
                if i == 0:
                    for c in range(DC):
                        dve.wait_ge(*m["x_hi"].next())
                        V.scalar_tensor_tensor(HL[:, c, :], h[:, c, :], col("norm_mix_1", c), HH[:, c, :].bitcast(f32),
                                               MUL, SUB).then_inc(*m["x_lo"].tick())
                for t in range(2):
                    dve.wait_ge(*landed(4, 2, t))
                    if i:
                        dve.wait_ge(*m["silu_ok"].next())
                    V.tensor_copy(pre[:, t, :], bank(t, 160)).then_inc(*m["tile_free"].tick())
                close(4, 2)
            for r in range(2):
                dve.wait_ge(*m["kc_hi"].next())
                V.tensor_tensor(of_head(KCL, r), of_group(ps[:, 6, 0:P], r), of_head(KCH, r).bitcast(f32), SUB)\
                 .then_inc(*m["kc_lo"].tick())
            dve.wait_ge(*m["acc_add"].upto())
            dve.wait_ge(*m["cmp_done"].next(2))
            V.tensor_copy(VC, ps[:, 5, 0:GR * HD]).then_inc(*m["vc_ok"].tick())
            for j in range(2):
                for t in range(4):
                    dve.wait_ge(*landed(4, 4, t))
                    if j:
                        dve.wait_ge(*m["q_lo"].upto())
                    V.scalar_tensor_tensor(qst[:, t, :], bank(t), SC2, rstd[:, :], MUL, MUL).then_inc(*m["tile_free"].tick())
                dve.wait_ge(*m["tile_free"].upto())
                for t in range(4):
                    c = 4 * j + t
                    lower(XL[:, c, :], qst[:, t, :], XH[:, c, :], m["q_hi"], m["q_lo"])
                close(4, 4)
            for t in range(TT):
                dve.wait_ge(*landed(1, 4, t))
                V.tensor_scalar(GT[:, t, :], bank(t, 48), small[:, 80 + t:81 + t], None, MUL).then_inc(*m["tile_free"].tick())
            close(1, 4)
            dve.wait_ge(*m["gate_s"].next())
            V.tensor_scalar(GT[:, 0, 0:48:3], GT[:, 0, 0:48:3], col("has_any"), None, MUL).then_inc(*m["gate_ok"].tick())
            for c in KEYS[:2]:
                lower(HL[:, c, :], K32[:, c, :], HH[:, c, :], m["krep_hi"], m["krep_lo"])
            dve.wait_ge(sems["bc_in"], 16 * GR)
            dve.wait_ge(*m["q_lo"].upto())
            for c in range(DC):
                dve.wait_ge(*m["c_lg"].next())
                V.tensor_copy(LT[64 * (c % 2):64 * (c % 2) + 64, c // 2, :], ps[0:64, (b.t + c) % 4, :])\
                 .then_inc(*m["tile_free"].tick())
            for g in range(GR):
                dve.wait_ge(*m["tile_free"].upto(2 * g - 6))
                V.tensor_tensor(LT[:, g, :], LT[:, g, :], bcs[:, g, :], ADD).then_inc(*m["lt_ok"].tick())
            dve.wait_ge(*m["cmp_done"].upto())
            b.t = 0

            def heads(x):
                return x.rearrange("p (k n) -> p k n", n=32)

            def spread(at):
                return small[:, at:at + H2].unsqueeze(2).to_broadcast([P, H2, 32])

            for t in range(TT):
                dve.wait_ge(*m["c_lg"].next())
                V.tensor_reduce(small[:, 96 + 16 * t:112 + 16 * t], heads(ps[:, t, :]), AX.X, MAX).then_inc(*m["c_mx"].tick())
            for t in range(TT):
                dve.wait_ge(*m["c_mx"].upto(t - 3))
                V.tensor_tensor(heads(L[:, t, :]), heads(ps[:, t, :]), spread(96 + 16 * t), SUB).then_inc(*m["tile_free"].tick())
            for c in KEYS[2:]:
                lower(HL[:, c, :], K32[:, c, :], HH[:, c, :], m["krep_hi"], m["krep_lo"])
            for t in range(TT):
                dve.wait_ge(*m["c_exp"].next())
                V.tensor_reduce(small[:, 160 + 16 * t:176 + 16 * t], heads(L[:, t, :]), AX.X, ADD).then_inc(*m["c_sum"].tick())
            dve.wait_ge(*m["c_sum"].upto())
            V.reciprocal(small[:, 160:224], small[:, 160:224]).then_inc(*m["c_inv"].tick())
            dve.wait_ge(*m["c_inv"].upto())
            dve.wait_ge(*m["gate_ok"].upto())
            for t in range(TT):
                gate = GT[:, t, 0:48:3]
                inv = small[:, 160 + 16 * t:176 + 16 * t]
                V.tensor_tensor(inv, inv, gate, MUL).then_inc(*m["c_inv"].tick())
            for t in range(TT):
                dve.wait_ge(*m["c_inv"].upto(t - 3))
                V.tensor_tensor(heads(L[:, t, :]), heads(L[:, t, :]), spread(160 + 16 * t), MUL).then_inc(*m["c_mul"].tick())
            dve.wait_ge(*m["c_tr"].next(TT))
            NJ = 2 * H2
            for n in range(NJ + 1):
                if n < NJ:
                    hd = n // 2
                    if n % 2 == 0:
                        dve.wait_ge(strip_in[hd % 3], 16 * (hd // 3 + 1))
                    logits(n, JOBS2[n])
                if n >= 1:
                    normalise(n - 1, JOBS2[n - 1])
                if n >= 7 and n % 4 == 3:
                    c = (n - 7) // 4
                    lower(XL[:, c, :], O2[:, c, :], XH[:, c, :], m["x_hi"], m["x_lo"])
            lower(XL[:, 7, :], O2[:, 7, :], XH[:, 7, :], m["x_hi"], m["x_lo"])
            m["t_done"].next(3 * NJ)
            residual(2, 4, 4, "norm_mlp_1")
            mlp(None)
            invert(rstd[:, :])
            dve.wait_ge(*m["norm_inv"].upto())
            for c in range(DC):
                V.scalar_tensor_tensor(h[:, c, :], h[:, c, :], col("final_norm", c), rstd[:, :], MUL, MUL)\
                 .then_inc(*m["out_ok"].tick())


def blocks(w, nu, nt, cols):
    w = w[:, cols]
    n, k = w.shape[1], w.shape[0] // (nu * P)
    assert n == nt * P or nt == 0
    out = np.zeros((nu, P, 1024), w.dtype)
    out[:, :, :k * n] = w.reshape(nu, k, P, n).transpose(0, 2, 1, 3).reshape(nu, P, k * n)
    return out


def kernel(**inputs):
    import concourse.bacc as _bacc
    from concourse.bass_utils import run_bass_kernel_spmd as _run

    a = {k: np.asarray(v) for k, v in inputs.items()}
    R = np.arange
    w = []
    wi = a["w_in"][0]
    wi = np.concatenate([wi, np.zeros((D, 64), wi.dtype)], 1)
    o3 = QR + KVR + ROPE
    pair = R(256)
    kr = QR + KVR + R(ROPE)
    zero = o3 + 2 * CC + R(64)
    rot = np.concatenate([zero, kr, kr[16:], kr[:16]])
    for cols in (o3 + pair, o3 + CC + pair, pair, np.concatenate([256 + R(P), rot]), o3 + 256 + pair,
                 QR + pair, o3 + CC + 256 + pair):
        w.append(blocks(wi, 2, 2, cols))
    q = a["w_q_b"][0]
    head = [np.concatenate([96 * i + R(96), 96 * i + 80 + R(16), 96 * i + 64 + R(16)]) for i in range(H1)]
    for i in range(0, H1, 2):
        w.append(blocks(q, 1, 2, np.concatenate(head[i:i + 2])))
    kv = a["w_kv_b"][0]
    w.append(blocks(kv, 1, 4, np.concatenate([128 * i + R(64) for i in range(H1)])))
    w.append(blocks(kv, 1, 0, np.concatenate([128 * i + 64 + R(64) for i in range(H1)])))

    def full(m, nu=2):
        for i in range(m.shape[1] // 256):
            w.append(blocks(m, nu, 2, 256 * i + pair))

    def quads(m):
        for i in range(m.shape[1] // 512):
            w.append(blocks(m, 4, 4, 512 * i + R(512)))

    quads(a["w_o"][0])
    for i in range(2):
        w.append(blocks(a["w_ple_proj"][0], 1, 4, 512 * i + R(512)))
    g, u, dn = a["w_ffn_gate"][0], a["w_ffn_up"][0], a["w_ffn_down"][0]

    def ffn_up(grp, pairs):
        for i in range(pairs):
            w.append(blocks(g, 2, 2, 512 * grp + 256 * i + pair))
            w.append(blocks(u, 2, 2, 512 * grp + 256 * i + pair))

    def down(m, grp):
        full(m[512 * grp:512 * grp + 512], 1)

    ffn_up(0, 2)
    for i in range(1, 5):
        ffn_up(i, 2)
        down(dn, i - 1)
    ffn_up(5, 1)
    down(dn, 4)
    for i in range(2):
        w.append(blocks(dn[2560:], 1, 4, 512 * i + R(512)))
    quads(a["w_ple_gate"][0])
    ai = a["a_w_in_2"][0]
    for i in range(4):
        for part in (1, 2, 0):
            w.append(blocks(ai, 2, 2, D * part + 256 * i + pair))
    quads(a["a_w_out_2"][0])

    def mlp(layer):
        w1, w2 = a["mlp_w1_2"][layer], a["mlp_w2_2"][layer]
        for i in range(9):
            if i < 8:
                full(w1[:, 512 * i:512 * i + 512])
            if i:
                down(w2, i - 1)

    mlp(0)
    full(a["w_kv_2"])
    for n in ("phi_k_w1_2", "phi_v_w1_2"):
        w.append(blocks(a[n], 4, 2, pair))
    quads(a["b_w_qg_2"][0][:, :D])
    w.append(blocks(a["b_w_qg_2"][0], 1, 0, D + R(48)))
    quads(a["b_w_o_2"][0])
    mlp(1)
    weights = np.concatenate(w)
    assert weights.shape[0] == NU, (weights.shape, NU)

    def cols(v):
        v = np.asarray(v, np.float32).reshape(-1, P)
        return v.T

    lane = np.arange(P)
    inv = (10000.0 ** (-np.arange(0, ROPE, 2, dtype=np.float64) / ROPE)).astype(np.float32)
    vals = dict(
        g_mix_pre=a["g_mix_pre"], g_q_a=a["g_q_a"], g_kv_a=a["g_kv_a"], conv_b=a["conv_b"], conv_ln_g=a["conv_ln_g"],
        conv_ln_b=a["conv_ln_b"], g_mix_post=a["g_mix_post"], g_ffn_pre=a["g_ffn_pre"], ffn_dw_b=a["ffn_dw_b"],
        g_ffn_post=a["g_ffn_post"], g_ple=a["g_ple"], norm_mix_0=a["norm_mix_2"][0], norm_mix_1=a["norm_mix_2"][1],
        norm_mlp_0=a["norm_mlp_2"][0], norm_mlp_1=a["norm_mlp_2"][1], kv_norm=a["kv_norm_2"],
        final_norm=a["final_norm_2"], conv_w=a["conv_w"], ffn_dw_w=a["ffn_dw_w"], a_conv_w=a["a_conv_w_2"],
        freq=np.tile(inv, 8), cosine=np.where(lane < 96, 0.25, 0.0), quarter=np.where(lane < 96, np.pi / 2, 0.0),
        sign=np.where((lane >= 96) & (lane < 112), -1.0, 1.0), has_any=(lane >= 31).astype(np.float32), pe_k=a["cmp_pe_k_2"],
        pe_v=a["cmp_pe_v_2"])
    vecs = np.concatenate([cols(vals[n]) for n, _ in VECS], 1)
    assert vecs.shape == (P, NV)
    key, query = np.arange(S)[None, :] - (S - P), np.arange(P)[:, None]
    mask = np.where(key <= query, 0.0, NEG).astype(np.float32)

    def one_hot(dist):
        d = np.maximum(dist, 0)
        large = 16 + (np.log(np.maximum(d, 1) / 16.0) / math.log(8.0) * 16 + 1e-9).astype(np.int32)
        bucket = np.where(dist < 0, 32, np.where(d < 16, d, np.minimum(large, 31)))
        return (np.arange(33)[:, None] == bucket[None, :]).astype(np.float32)

    onehots = np.concatenate([one_hot(511 - R(640)), one_hot(R(1040) - 527)], 1)
    rb = np.concatenate([a["rel_bias_2"], np.full((1, H2), NEG, np.float32)])

    def by_chunk(w):
        return w.reshape(2, P, HD).transpose(1, 0, 2)

    k2, v2 = by_chunk(a["phi_k_w2_2"]), by_chunk(a["phi_v_w2_2"])
    w2 = np.concatenate([np.concatenate([k2, k2], 2).reshape(P, 256), v2.reshape(P, P)], 1)

    ins = dict(onehots=onehots, relb=rb, w2=w2, xT=a["x"][0].T, pT=a["p"][0, 0].T, positions=a["positions"], weights=weights, vecs=vecs,
               mask=mask, ident=np.eye(P, dtype=np.float32))
    nc = _bacc.Bacc("TRN2", target_bir_lowering=False, num_devices=1)
    io, arrays = {}, {}
    for name, v in ins.items():
        arrays["in_" + name] = np.ascontiguousarray(v)
        io[name] = nc.dram_tensor("in_" + name, v.shape, mybir.dt.from_np(v.dtype), kind="ExternalInput").ap()
    io["tab"] = nc.dram_tensor("tab", (H2, P, 640), mybir.dt.float32, kind="Internal").ap()
    io["ftab"] = nc.dram_tensor("ftab", (H2, 32, 1040), mybir.dt.float32, kind="Internal").ap()
    io["out"] = nc.dram_tensor("out_T", (D, S), mybir.dt.float32, kind="ExternalOutput").ap()
    build(nc, io)
    r = _run(nc, [arrays], core_ids=[0])
    return r.results[0]["out_T"].T.reshape(1, S, D)
```
